# Optimizing a Trainium2 kernel written in Bass

```python
import jax, jax.numpy as jnp
from jax import lax
import numpy as np

D_MODEL = 1024
BATCH = 1
SEQ = 256
DEPTH = 2

MLA_HEADS = 8
MLA_Q_RANK = 256
MLA_KV_RANK = 128
MLA_NOPE = 64
MLA_ROPE = 32
MLA_V = 64
MOBA_HEADS = 8
MOBA_HEAD_DIM = 64
MOBA_BLOCK = 256
MOBA_TOPK = 3
MOBA_Q_CHUNK = 32
RET_HEADS = 4
RET_QK_DIM = 64
RET_V_DIM = 128
RET_CHUNK = 128
RET_THETA = 10000.0
ROPE_THETA = 500000.0
PARTIAL_ROPE_DIV = 4
ATTN_Q_BLOCK = 128
D_FF = 4 * D_MODEL
NORM_EPS = 1e-6
GN_EPS = 1e-5
NEG_INF = -1e30

MOBA_W = MOBA_HEADS * MOBA_HEAD_DIM
RET_QK_W = RET_HEADS * RET_QK_DIM
RET_V_W = RET_HEADS * RET_V_DIM
MLA_OUT_W = MLA_HEADS * MLA_V
IN_SPLIT_SIZES = (MLA_Q_RANK, MLA_KV_RANK, MLA_ROPE,
                  MOBA_W, MOBA_W, MOBA_W,
                  RET_QK_W, RET_QK_W, RET_V_W, RET_V_W,
                  D_MODEL, D_MODEL, D_MODEL)
IN_COLS = sum(IN_SPLIT_SIZES)
IN_SPLIT_IDX = tuple(int(i) for i in np.cumsum(IN_SPLIT_SIZES)[:-1])


def rms_norm(x, g, eps=NORM_EPS):
    xf = x.astype(jnp.float32)
    y = xf * lax.rsqrt(jnp.mean(xf * xf, axis=-1, keepdims=True) + eps)
    return (y * g.astype(jnp.float32)).astype(x.dtype)

def rope_tables(seq, dim, theta):
    inv = 1.0 / (theta ** (jnp.arange(0, dim, 2, dtype=jnp.float32) / dim))
    ang = jnp.arange(seq, dtype=jnp.float32)[:, None] * inv[None, :]
    return jnp.cos(ang), jnp.sin(ang)

def apply_rope(x, cos, sin):
    half = x.shape[-1] // 2
    x1, x2 = x[..., :half], x[..., half:]
    c, s = cos.astype(x.dtype), sin.astype(x.dtype)
    return jnp.concatenate([x1 * c - x2 * s, x1 * s + x2 * c], axis=-1)

def causal_attention(q, k, v, scale):
    B, H, S, _ = q.shape
    kpos = jnp.arange(S)

    def block(i):
        start = i * ATTN_Q_BLOCK
        qb = lax.dynamic_slice_in_dim(q, start, ATTN_Q_BLOCK, axis=2)
        s = jnp.einsum('bhqd,bhkd->bhqk', qb, k).astype(jnp.float32) * scale
        qpos = start + jnp.arange(ATTN_Q_BLOCK)
        s = jnp.where(kpos[None, :] <= qpos[:, None], s, NEG_INF)
        p = jax.nn.softmax(s, axis=-1).astype(v.dtype)
        return jnp.einsum('bhqk,bhkd->bhqd', p, v)

    o = lax.map(block, jnp.arange(S // ATTN_Q_BLOCK))
    return o.transpose(1, 2, 0, 3, 4).reshape(B, H, S, v.shape[-1])

def mla_branch(cq, ckv, k_rope, q_norm_g, kv_norm_g, w_q_up, w_kv_up, cos, sin):
    B, S, _ = cq.shape
    cq = rms_norm(cq, q_norm_g)
    ckv = rms_norm(ckv, kv_norm_g)
    q = (cq @ w_q_up).reshape(B, S, MLA_HEADS, MLA_NOPE + MLA_ROPE).transpose(0, 2, 1, 3)
    q = jnp.concatenate([q[..., :MLA_NOPE], apply_rope(q[..., MLA_NOPE:], cos, sin)], axis=-1)
    kv = (ckv @ w_kv_up).reshape(B, S, MLA_HEADS, MLA_NOPE + MLA_V).transpose(0, 2, 1, 3)
    k_pe = apply_rope(k_rope, cos, sin)[:, None]
    k = jnp.concatenate([kv[..., :MLA_NOPE],
                         jnp.broadcast_to(k_pe, (B, MLA_HEADS, S, MLA_ROPE))], axis=-1)
    v = kv[..., MLA_NOPE:]
    o = causal_attention(q, k, v, (MLA_NOPE + MLA_ROPE) ** -0.5)
    return o.transpose(0, 2, 1, 3).reshape(B, S, MLA_OUT_W)

def moba_branch(q, k, v, cos, sin):
    B, S, _ = q.shape
    H, Dh, BS, QC = MOBA_HEADS, MOBA_HEAD_DIM, MOBA_BLOCK, MOBA_Q_CHUNK
    rd = Dh // PARTIAL_ROPE_DIV

    def heads(t):
        return t.reshape(B, S, H, Dh).transpose(0, 2, 1, 3)

    def partial_rope(t):
        return jnp.concatenate([apply_rope(t[..., :rd], cos, sin), t[..., rd:]], axis=-1)

    q, k, v = partial_rope(heads(q)), partial_rope(heads(k)), heads(v)
    nb = -(-S // BS)
    pad = nb * BS - S
    padw = ((0, 0), (0, 0), (0, pad), (0, 0))
    q, k, v = jnp.pad(q, padw), jnp.pad(k, padw), jnp.pad(v, padw)
    kb = k.reshape(B, H, nb, BS, Dh)
    vb = v.reshape(B, H, nb, BS, Dh)
    k_mean = jnp.mean(kb.astype(jnp.float32), axis=3)
    topk = min(MOBA_TOPK, nb)
    scale = Dh ** -0.5
    bi = jnp.arange(B)[:, None, None, None]
    hi = jnp.arange(H)[None, :, None, None]

    def chunk(c):
        start = c * QC
        blk = start // BS
        qc = lax.dynamic_slice_in_dim(q, start, QC, axis=2)
        gate = jnp.einsum('bhqd,bhnd->bhqn', qc.astype(jnp.float32), k_mean)
        gate = jnp.where(jnp.arange(nb) < blk, gate, NEG_INF)
        _, idx = lax.top_k(gate, topk)
        sel_valid = jnp.arange(topk) < blk
        k_sel = kb[bi, hi, idx]
        v_sel = vb[bi, hi, idx]
        s_sel = jnp.einsum('bhqd,bhqnkd->bhqnk', qc, k_sel).astype(jnp.float32) * scale
        s_sel = jnp.where(sel_valid[:, None], s_sel, NEG_INF).reshape(B, H, QC, topk * BS)
        k_own = lax.dynamic_index_in_dim(kb, blk, axis=2, keepdims=False)
        v_own = lax.dynamic_index_in_dim(vb, blk, axis=2, keepdims=False)
        s_own = jnp.einsum('bhqd,bhkd->bhqk', qc, k_own).astype(jnp.float32) * scale
        qpos = start + jnp.arange(QC)
        kpos = blk * BS + jnp.arange(BS)
        s_own = jnp.where(kpos[None, :] <= qpos[:, None], s_own, NEG_INF)
        p = jax.nn.softmax(jnp.concatenate([s_sel, s_own], axis=-1), axis=-1).astype(v.dtype)
        o_sel = jnp.einsum('bhqn,bhqnd->bhqd', p[..., :topk * BS],
                           v_sel.reshape(B, H, QC, topk * BS, Dh))
        o_own = jnp.einsum('bhqk,bhkd->bhqd', p[..., topk * BS:], v_own)
        return o_sel + o_own

    o = lax.map(chunk, jnp.arange(nb * BS // QC))
    o = o.transpose(1, 2, 0, 3, 4).reshape(B, H, nb * BS, Dh)[:, :, :S]
    return o.transpose(0, 2, 1, 3).reshape(B, S, MOBA_W)

def retention_branch(q, k, v, g, gn_w, gn_b, cos, sin):
    B, S, _ = q.shape
    H, Dk, Dv, C = RET_HEADS, RET_QK_DIM, RET_V_DIM, RET_CHUNK
    nc = S // C
    f32 = jnp.float32
    q = apply_rope(q.astype(f32).reshape(B, S, H, Dk).transpose(0, 2, 1, 3), cos, sin)
    k = apply_rope(k.astype(f32).reshape(B, S, H, Dk).transpose(0, 2, 1, 3), cos, sin) * (Dk ** -0.5)
    v = v.astype(f32).reshape(B, S, H, Dv).transpose(0, 2, 1, 3)
    log_gamma = jnp.log(1.0 - 2.0 ** (-5.0 - jnp.arange(H, dtype=f32)))
    pos = jnp.arange(C, dtype=f32)
    diff = pos[:, None] - pos[None, :]
    decay_in = jnp.where(diff >= 0, jnp.exp(log_gamma[:, None, None] * diff), 0.0)
    xi = jnp.exp(log_gamma[:, None] * (pos + 1.0))
    zeta = jnp.exp(log_gamma[:, None] * (C - 1.0 - pos))
    gamma_c = jnp.exp(log_gamma * C)[None, :, None, None]
    qc = q.reshape(B, H, nc, C, Dk)
    kc = k.reshape(B, H, nc, C, Dk)
    vc = v.reshape(B, H, nc, C, Dv)
    scores = jnp.einsum('bhnid,bhnjd->bhnij', qc, kc) * decay_in[:, None]
    inner = jnp.einsum('bhnij,bhnje->bhnie', scores, vc)
    kv_chunk = jnp.einsum('bhnjd,bhnje->bhnde', kc * zeta[:, None, :, None], vc)

    def step(R, kv):
        return gamma_c * R + kv, R

    _, R_prev = lax.scan(step, jnp.zeros((B, H, Dk, Dv), f32), kv_chunk.transpose(2, 0, 1, 3, 4))
    R_prev = R_prev.transpose(1, 2, 0, 3, 4)
    cross = jnp.einsum('bhnid,bhnde->bhnie', qc * xi[:, None, :, None], R_prev)
    o = (inner + cross).reshape(B, H, S, Dv)
    mu = jnp.mean(o, axis=-1, keepdims=True)
    var = jnp.mean(jnp.square(o - mu), axis=-1, keepdims=True)
    o = (o - mu) * lax.rsqrt(var + GN_EPS)
    o = o.transpose(0, 2, 1, 3).reshape(B, S, RET_V_W) * gn_w.astype(f32) + gn_b.astype(f32)
    return jax.nn.silu(g) * o.astype(g.dtype)

def hybrid_mixer(h, w_in, mla_q_norm, mla_kv_norm, mla_w_q_up, mla_w_kv_up, ret_gn_w, ret_gn_b,
                 w_branch_mla, w_branch_moba, w_branch_ret, w_out, ropes):
    (cos_mla, sin_mla), (cos_moba, sin_moba), (cos_ret, sin_ret) = ropes
    p = h @ w_in
    (cq, ckv, k_rope, mq, mk, mv, rq, rk, rv, rg, g_mla, g_moba, g_ret) = jnp.split(p, IN_SPLIT_IDX, axis=-1)
    o_mla = mla_branch(cq, ckv, k_rope, mla_q_norm, mla_kv_norm, mla_w_q_up, mla_w_kv_up, cos_mla, sin_mla)
    o_moba = moba_branch(mq, mk, mv, cos_moba, sin_moba)
    o_ret = retention_branch(rq, rk, rv, rg, ret_gn_w, ret_gn_b, cos_ret, sin_ret)
    merged = (jax.nn.sigmoid(g_mla) * (o_mla @ w_branch_mla)
              + jax.nn.sigmoid(g_moba) * (o_moba @ w_branch_moba)
              + jax.nn.sigmoid(g_ret) * (o_ret @ w_branch_ret))
    return merged @ w_out

def squared_relu_mlp(h, w_up, w_down):
    return jnp.square(jax.nn.relu(h @ w_up)) @ w_down

def first_inputs(seed: int = 0) -> dict:
    key = jax.random.key(seed)
    ks = jax.random.split(key, 18)

    def dense(k, shape):
        return jax.random.normal(k, shape, jnp.float32) * (shape[-2] ** -0.5)

    def gain(k, shape):
        return 1.0 + 0.02 * jax.random.normal(k, shape, jnp.float32)

    L = DEPTH
    return {
        "x": jax.random.normal(ks[0], (BATCH, SEQ, D_MODEL), jnp.float32),
        "attn_norm": gain(ks[1], (L, D_MODEL)),
        "w_in": dense(ks[2], (L, D_MODEL, IN_COLS)),
        "mla_q_norm": gain(ks[3], (L, MLA_Q_RANK)),
        "mla_kv_norm": gain(ks[4], (L, MLA_KV_RANK)),
        "mla_w_q_up": dense(ks[5], (L, MLA_Q_RANK, MLA_HEADS * (MLA_NOPE + MLA_ROPE))),
        "mla_w_kv_up": dense(ks[6], (L, MLA_KV_RANK, MLA_HEADS * (MLA_NOPE + MLA_V))),
        "ret_gn_w": gain(ks[7], (L, RET_V_W)),
        "ret_gn_b": 0.02 * jax.random.normal(ks[8], (L, RET_V_W), jnp.float32),
        "w_branch_mla": dense(ks[9], (L, MLA_OUT_W, D_MODEL)),
        "w_branch_moba": dense(ks[10], (L, MOBA_W, D_MODEL)),
        "w_branch_ret": dense(ks[11], (L, RET_V_W, D_MODEL)),
        "w_out": dense(ks[12], (L, D_MODEL, D_MODEL)),
        "mlp_norm": gain(ks[13], (L, D_MODEL)),
        "w_mlp_up": dense(ks[14], (L, D_MODEL, D_FF)),
        "w_mlp_down": dense(ks[15], (L, D_FF, D_MODEL)),
        "final_norm": gain(ks[16], (D_MODEL,)),
    }

def first_block(x, attn_norm, w_in, mla_q_norm, mla_kv_norm, mla_w_q_up, mla_w_kv_up, ret_gn_w, ret_gn_b,
              w_branch_mla, w_branch_moba, w_branch_ret, w_out, mlp_norm, w_mlp_up, w_mlp_down, final_norm):
    S = x.shape[1]
    ropes = (rope_tables(S, MLA_ROPE, ROPE_THETA),
             rope_tables(S, MOBA_HEAD_DIM // PARTIAL_ROPE_DIV, ROPE_THETA),
             rope_tables(S, RET_QK_DIM, RET_THETA))
    for l in range(DEPTH):
        h = rms_norm(x, attn_norm[l])
        x = x + hybrid_mixer(h, w_in[l], mla_q_norm[l], mla_kv_norm[l], mla_w_q_up[l], mla_w_kv_up[l],
                             ret_gn_w[l], ret_gn_b[l], w_branch_mla[l], w_branch_moba[l], w_branch_ret[l],
                             w_out[l], ropes)
        h = rms_norm(x, mlp_norm[l])
        x = x + squared_relu_mlp(h, w_mlp_up[l], w_mlp_down[l])
    return rms_norm(x, final_norm)


GRID_W = 64
PLE_DIM = 256
EPS = 1e-6
GLA_HEADS = 4
GLA_DK = 128
GLA_DV = 256
GLA_KEY = GLA_HEADS * GLA_DK
GLA_VAL = GLA_HEADS * GLA_DV
GLA_RANK = 16
GLA_TAU = 16.0
GLA_CHUNK = 64
ATTN_HEADS = 8
ATTN_KV_HEADS = 2
HEAD_DIM = 128
ATTN_Q = ATTN_HEADS * HEAD_DIM
ATTN_KV = ATTN_KV_HEADS * HEAD_DIM
Q_BLOCK = 128
ROPE_THETA_2 = 10000.0
ROPE_AXIS_DIM = HEAD_DIM // 2
FFN_HIDDEN = -(-8 * D_MODEL // (3 * 256)) * 256
IN_SPLITS = (GLA_KEY, GLA_KEY, GLA_VAL, GLA_VAL, GLA_RANK, GLA_RANK,
             ATTN_Q, ATTN_KV, ATTN_KV, D_MODEL, D_MODEL)
IN_WIDTH = sum(IN_SPLITS)


def rms_norm_2(x, g):
    xf = x.astype(jnp.float32)
    y = xf * lax.rsqrt(jnp.mean(xf * xf, axis=-1, keepdims=True) + EPS)
    return (y * g.astype(jnp.float32)).astype(x.dtype)

def axial_rope_tables(seq_len):
    rows = seq_len // GRID_W
    row = jnp.repeat(jnp.arange(rows, dtype=jnp.float32), GRID_W)
    col = jnp.tile(jnp.arange(GRID_W, dtype=jnp.float32), rows)
    inv = ROPE_THETA_2 ** (-jnp.arange(0, ROPE_AXIS_DIM, 2, dtype=jnp.float32) / ROPE_AXIS_DIM)
    ang = jnp.stack([row[:, None] * inv, col[:, None] * inv], axis=1)
    return jnp.cos(ang), jnp.sin(ang)

def apply_axial_rope(x, cos, sin):
    b, s, h, d = x.shape
    xr = x.astype(jnp.float32).reshape(b, s, h, 2, 2, d // 4)
    c = cos[None, :, None]
    sn = sin[None, :, None]
    x1, x2 = xr[..., 0, :], xr[..., 1, :]
    out = jnp.stack([x1 * c - x2 * sn, x2 * c + x1 * sn], axis=-2)
    return out.reshape(b, s, h, d).astype(x.dtype)

def gla_chunked(q, k, v, log_a):
    b, s, h, dk = q.shape
    dv = v.shape[-1]
    n = s // GLA_CHUNK
    c = GLA_CHUNK

    def chunks(t):
        return t.reshape(b, n, c, h, t.shape[-1]).transpose(1, 0, 3, 2, 4)

    q, k, v, la = chunks(q), chunks(k), chunks(v), chunks(log_a)
    cum = jnp.cumsum(la, axis=3)
    last = cum[:, :, :, -1:, :]
    q_dec = q * jnp.exp(cum)
    k_intra = k * jnp.exp(-cum)
    k_state = k * jnp.exp(last - cum)
    mask = jnp.tril(jnp.ones((c, c), dtype=bool))
    scores = jnp.where(mask, jnp.einsum('nbhid,nbhjd->nbhij', q_dec, k_intra), 0.0)
    o_intra = jnp.einsum('nbhij,nbhjv->nbhiv', scores, v)

    def step(state, xs):
        qd, ks, vc, lst = xs
        o = jnp.einsum('bhid,bhdv->bhiv', qd, state)
        state = state * jnp.exp(lst[:, :, 0, :])[..., None] + jnp.einsum('bhjd,bhjv->bhdv', ks, vc)
        return state, o

    s0 = jnp.zeros((b, h, dk, dv), jnp.float32)
    _, o_inter = lax.scan(step, s0, (q_dec, k_state, v, last))
    o = o_intra + o_inter
    return o.transpose(1, 0, 3, 2, 4).reshape(b, s, h, dv)

def gqa_attention(q, k, v):
    b, s, hq, hd = q.shape
    hkv = k.shape[2]
    g = hq // hkv
    nb = s // Q_BLOCK
    qb = q.reshape(b, nb, Q_BLOCK, hkv, g, hd).transpose(1, 0, 2, 3, 4, 5)
    scale = hd ** -0.5

    def block(qblk):
        sc = jnp.einsum('bqkgd,bskd->bkgqs', qblk, k).astype(jnp.float32) * scale
        pr = jax.nn.softmax(sc, axis=-1).astype(v.dtype)
        return jnp.einsum('bkgqs,bskd->bqkgd', pr, v)

    out = lax.map(block, qb)
    return out.transpose(1, 0, 2, 3, 4, 5).reshape(b, s, hq * hd)

def hybrid_layer(h, p_i, cos, sin, g_mix_pre, w_in, w_alpha_up, b_alpha, g_gla_out,
                 g_q_norm, g_k_norm, w_o_gla, w_o_attn, w_out, g_mix_post,
                 g_ffn_pre, w_ffn_in, w_ffn_out, g_ffn_post, w_ple_proj, w_ple_gate, g_ple_post):
    b, s, _ = h.shape
    f32 = jnp.float32
    u = rms_norm_2(h, g_mix_pre)
    offsets = np.cumsum(IN_SPLITS)[:-1].tolist()
    (gq, gk, gv, gg, ra_f, ra_b, aq, ak, av, gate_a, gate_b) = jnp.split(u @ w_in, offsets, axis=-1)

    qh = gq.astype(f32).reshape(b, s, GLA_HEADS, GLA_DK) * (GLA_DK ** -0.5)
    kh = gk.astype(f32).reshape(b, s, GLA_HEADS, GLA_DK)
    vh = gv.astype(f32).reshape(b, s, GLA_HEADS, GLA_DV)
    la_f = (jax.nn.log_sigmoid(ra_f.astype(f32) @ w_alpha_up[0].astype(f32) + b_alpha[0].astype(f32))
            / GLA_TAU).reshape(b, s, GLA_HEADS, GLA_DK)
    la_b = (jax.nn.log_sigmoid(ra_b.astype(f32) @ w_alpha_up[1].astype(f32) + b_alpha[1].astype(f32))
            / GLA_TAU).reshape(b, s, GLA_HEADS, GLA_DK)
    o_f = gla_chunked(qh, kh, vh, la_f)
    o_b = gla_chunked(qh[:, ::-1], kh[:, ::-1], vh[:, ::-1], la_b[:, ::-1])[:, ::-1]
    o_gla = rms_norm_2(o_f + o_b, g_gla_out).reshape(b, s, GLA_VAL).astype(h.dtype)
    branch_a = (o_gla * jax.nn.silu(gg)) @ w_o_gla

    q = apply_axial_rope(rms_norm_2(aq.reshape(b, s, ATTN_HEADS, HEAD_DIM), g_q_norm), cos, sin)
    k = apply_axial_rope(rms_norm_2(ak.reshape(b, s, ATTN_KV_HEADS, HEAD_DIM), g_k_norm), cos, sin)
    v = av.reshape(b, s, ATTN_KV_HEADS, HEAD_DIM)
    branch_b = gqa_attention(q, k, v) @ w_o_attn

    mixed = jax.nn.sigmoid(gate_a) * branch_a + jax.nn.sigmoid(gate_b) * branch_b
    h = h + rms_norm_2(mixed @ w_out, g_mix_post)

    gate, up = jnp.split(rms_norm_2(h, g_ffn_pre) @ w_ffn_in, 2, axis=-1)
    h = h + rms_norm_2((jax.nn.silu(gate) * up) @ w_ffn_out, g_ffn_post)

    e = p_i @ w_ple_proj
    h = h + rms_norm_2(jax.nn.sigmoid(h @ w_ple_gate) * e, g_ple_post)
    return h

def second_inputs(seed: int = 0) -> dict:
    key = jax.random.key(seed)
    ks = jax.random.split(key, 24)
    f32 = jnp.float32

    def w(k, shape, fan_in):
        return jax.random.normal(k, shape, f32) * (fan_in ** -0.5)

    def gain(k, shape):
        return 1.0 + 0.05 * jax.random.normal(k, shape, f32)

    return {
        "x": jax.random.normal(ks[0], (BATCH, SEQ, D_MODEL), f32),
        "p": jax.random.normal(ks[1], (DEPTH, BATCH, SEQ, PLE_DIM), f32),
        "g_mix_pre": gain(ks[2], (DEPTH, D_MODEL)),
        "w_in": w(ks[3], (DEPTH, D_MODEL, IN_WIDTH), D_MODEL),
        "w_alpha_up": w(ks[4], (DEPTH, 2, GLA_RANK, GLA_KEY), GLA_RANK),
        "b_alpha": 1.0 + 0.1 * jax.random.normal(ks[5], (DEPTH, 2, GLA_KEY), f32),
        "g_gla_out": gain(ks[6], (DEPTH, GLA_DV)),
        "g_q_norm": gain(ks[7], (DEPTH, HEAD_DIM)),
        "g_k_norm": gain(ks[8], (DEPTH, HEAD_DIM)),
        "w_o_gla": w(ks[9], (DEPTH, GLA_VAL, D_MODEL), GLA_VAL),
        "w_o_attn": w(ks[10], (DEPTH, ATTN_Q, D_MODEL), ATTN_Q),
        "w_out": w(ks[11], (DEPTH, D_MODEL, D_MODEL), D_MODEL),
        "g_mix_post": gain(ks[12], (DEPTH, D_MODEL)),
        "g_ffn_pre": gain(ks[13], (DEPTH, D_MODEL)),
        "w_ffn_in": w(ks[14], (DEPTH, D_MODEL, 2 * FFN_HIDDEN), D_MODEL),
        "w_ffn_out": w(ks[15], (DEPTH, FFN_HIDDEN, D_MODEL), FFN_HIDDEN),
        "g_ffn_post": gain(ks[16], (DEPTH, D_MODEL)),
        "w_ple_proj": w(ks[17], (DEPTH, PLE_DIM, D_MODEL), PLE_DIM),
        "w_ple_gate": w(ks[18], (DEPTH, D_MODEL, D_MODEL), D_MODEL),
        "g_ple_post": gain(ks[19], (DEPTH, D_MODEL)),
    }

def second_block(x, p, g_mix_pre, w_in, w_alpha_up, b_alpha, g_gla_out, g_q_norm, g_k_norm,
              w_o_gla, w_o_attn, w_out, g_mix_post, g_ffn_pre, w_ffn_in, w_ffn_out,
              g_ffn_post, w_ple_proj, w_ple_gate, g_ple_post):
    cos, sin = axial_rope_tables(x.shape[1])
    h = x
    for i in range(DEPTH):
        h = hybrid_layer(h, p[i], cos, sin, g_mix_pre[i], w_in[i], w_alpha_up[i], b_alpha[i],
                         g_gla_out[i], g_q_norm[i], g_k_norm[i], w_o_gla[i], w_o_attn[i],
                         w_out[i], g_mix_post[i], g_ffn_pre[i], w_ffn_in[i], w_ffn_out[i],
                         g_ffn_post[i], w_ple_proj[i], w_ple_gate[i], g_ple_post[i])
    return h


def setup_inputs(seed=0):
    out = dict(first_inputs(seed))
    for name, value in second_inputs(seed + 1).items():
        if name != "x":
            out[name + "_2"] = value
    return out


def reference(
    x, attn_norm, w_in, mla_q_norm, mla_kv_norm, mla_w_q_up, mla_w_kv_up, ret_gn_w, ret_gn_b,
    w_branch_mla, w_branch_moba, w_branch_ret, w_out, mlp_norm, w_mlp_up, w_mlp_down,
    final_norm, p_2, g_mix_pre_2, w_in_2, w_alpha_up_2, b_alpha_2, g_gla_out_2, g_q_norm_2,
    g_k_norm_2, w_o_gla_2, w_o_attn_2, w_out_2, g_mix_post_2, g_ffn_pre_2, w_ffn_in_2,
    w_ffn_out_2, g_ffn_post_2, w_ple_proj_2, w_ple_gate_2, g_ple_post_2,
):
    x = first_block(
        x, attn_norm, w_in, mla_q_norm, mla_kv_norm, mla_w_q_up, mla_w_kv_up, ret_gn_w,
        ret_gn_b, w_branch_mla, w_branch_moba, w_branch_ret, w_out, mlp_norm, w_mlp_up,
        w_mlp_down, final_norm,
    )
    return second_block(
        x, p_2, g_mix_pre_2, w_in_2, w_alpha_up_2, b_alpha_2, g_gla_out_2, g_q_norm_2,
        g_k_norm_2, w_o_gla_2, w_o_attn_2, w_out_2, g_mix_post_2, g_ffn_pre_2, w_ffn_in_2,
        w_ffn_out_2, g_ffn_post_2, w_ple_proj_2, w_ple_gate_2, g_ple_post_2,
    )


_drawn_inputs = setup_inputs


def setup_inputs(seed=0):
    import zlib

    import numpy as np

    out = dict(_drawn_inputs(seed))
    spreads = {}
    factors = {'mla_q_norm': 8.0,
     'mla_kv_norm': 5.047,
     'ret_gn_w': 3.911,
     'ret_gn_b': 3.734,
     'g_q_norm_2': 8.0,
     'g_k_norm_2': 8.0}
    for name, (base, spread) in spreads.items():
        noise = np.random.default_rng([zlib.crc32(name.encode()), seed]).standard_normal(out[name].shape)
        drawn = base * np.exp(spread * noise) if base else spread * noise
        out[name] = __import__('jax').numpy.asarray(drawn.astype(out[name].dtype))
    for name, factor in factors.items():
        out[name] = (out[name] * factor).astype(out[name].dtype)
    return out
```

```python
from contextlib import ExitStack

import numpy as np

import concourse.bass as bass
from concourse import mybir

F32 = mybir.dt.float32
F32R = mybir.dt.float32r
ALU = mybir.AluOpType
ACT = mybir.ActivationFunctionType
AX = mybir.AxisListType

P = 128
TOK = 256
NT = TOK // P
D = 1024
KD = D // P
LAYERS = 2
COLS = 512

MLA_H, MLA_Q, MLA_KV, NOPE, ROPE, MLA_V = 8, 256, 128, 64, 32, 64
QK_D = NOPE + ROPE
MOBA_H, MOBA_D = 8, 64
MOBA_R = MOBA_D // 4
RET_H, RET_K, RET_V, RET_CHUNK = 4, 64, 128, 128
D_FF = 4 * D
IN1 = [MLA_Q, MLA_KV, ROPE] + [MOBA_H * MOBA_D] * 3 + [RET_H * RET_K] * 2 + [RET_H * RET_V] * 2 + [D] * 3
CQ, CKV, KR, MQ, MK, MV, RQ, RK, RV, RG, G_MLA, G_MOBA, G_RET = [int(sum(IN1[:i])) for i in range(len(IN1))]
IN1_COLS = sum(IN1)

GLA_H, GLA_K, GLA_V, GLA_R, GLA_CHUNK = 4, 128, 256, 16, 64
GLA_TAU = 16.0
AQ_H, AKV_H, A_D, GRID_W = 8, 2, 128, 64
FFN = 2816
PLE = 256
IN2 = [GLA_H * GLA_K] * 2 + [GLA_H * GLA_V] * 2 + [GLA_R] * 2 + [AQ_H * A_D, AKV_H * A_D, AKV_H * A_D, D, D]
GQ, GK, GV, GG, RA_F, RA_B, AQ, AK, AV, G_A, G_B = [int(sum(IN2[:i])) for i in range(len(IN2))]
IN2_COLS = sum(IN2)
RA = IN2_COLS - 2 * GLA_R


def at2(col):
    return col if col < RA_F else col - 2 * GLA_R


NORM_EPS, GN_EPS = 1e-6, 1e-5
NEG = -1e30

CONST_PARTS = [[
    ("ident", 128), ("causal", 384), ("decay", RET_H * 384),
    ("c_mla", NT * 16), ("s_mla", NT * 16), ("c_moba", NT * 8), ("s_moba", NT * 8),
    ("c_ret", NT * 32), ("s_ret", NT * 32),
], [
    ("ident", 128), ("c_ax", NT * 64), ("s_ax", NT * 64),
    ("cum_f", 128), ("cum_b", 128), ("rest_f", 128), ("rest_b", 128), ("in_f", 128), ("in_b", 128), ("halves", 2),
]]
CONST_AT = {n: (sum(w for _, w in part[:i]), w) for part in CONST_PARTS for i, (n, w) in enumerate(part)}
CONST_COLS = [sum(w for _, w in part) for part in CONST_PARTS]


def constants():
    f = np.float32
    j, i = np.arange(P)[:, None], np.arange(P)[None, :]
    out = {"ident": np.eye(P, dtype=f)}
    tri = np.where(i <= j, 0.0, NEG).astype(f)
    out["causal"] = np.concatenate([np.zeros((P, P), f), tri, tri], 1)
    lg = np.log(1.0 - 2.0 ** (-5.0 - np.arange(RET_H)))
    wide = np.arange(TOK)[None, :] - np.arange(P)[:, None]
    dec = [np.where(wide >= 0, np.exp(g * np.maximum(wide, 0)), 0.0) * RET_K ** -0.5 for g in lg]
    out["decay"] = np.concatenate([np.concatenate([d, d[:, :P]], 1) for d in dec], 1)

    def rope(dim, theta):
        inv = (1.0 / (f(theta) ** (np.arange(0, dim, 2, dtype=f) / f(dim)))).astype(f)
        ang = (np.arange(TOK, dtype=f)[:, None] * inv[None, :]).astype(f)
        return np.cos(ang), np.sin(ang)

    def by_tile(a):
        return a.reshape(NT, P, -1).transpose(1, 0, 2).reshape(P, -1)

    for n, dim, theta in (("mla", ROPE, 500000.0), ("moba", MOBA_R, 500000.0), ("ret", RET_K, 10000.0)):
        c, s = rope(dim, theta)
        out["c_" + n], out["s_" + n] = by_tile(c), by_tile(s)
    axis = A_D // 2
    row = np.repeat(np.arange(TOK // GRID_W, dtype=f), GRID_W)
    col = np.tile(np.arange(GRID_W, dtype=f), TOK // GRID_W)
    inv = (f(10000.0) ** (-np.arange(0, axis, 2, dtype=f) / f(axis))).astype(f)
    ang = np.stack([row[:, None] * inv, col[:, None] * inv], 1)
    out["c_ax"], out["s_ax"] = by_tile(np.cos(ang)), by_tile(np.sin(ang))
    same = (j // GLA_CHUNK) == (i // GLA_CHUNK)
    out["cum_f"], out["cum_b"] = same * (j <= i) / GLA_TAU, same * (j >= i) / GLA_TAU
    out["rest_f"], out["rest_b"] = same * (j > i) / GLA_TAU, same * (j < i) / GLA_TAU
    out["in_f"], out["in_b"] = same * (j <= i), same * (j >= i)
    out["halves"] = (j // GLA_CHUNK == np.arange(P // GLA_CHUNK)[None, :]) / GLA_TAU
    return [np.ascontiguousarray(np.concatenate([np.asarray(out[n], f) for n, _ in part], 1)) for part in CONST_PARTS]


RING = 4


class Chunk:
    def __init__(self, name, weight, act, k_tiles, col, n, wide=False, to=0):
        self.name, self.weight, self.act, self.k_tiles = name, weight, act, k_tiles
        self.col, self.n, self.wide, self.to = col, n, wide, to
        self.units = k_tiles if wide or k_tiles == 1 else k_tiles // 2


def chunks_first():
    c = [Chunk("p", "w_in", "xT", KD, 0, MQ, to=0)]
    c += [Chunk("p", "w_in", "xT", KD, x, COLS, to=x) for x in range(MQ, G_MLA, COLS)]
    c += [Chunk("q_up", "mla_w_q_up", "cT", 2, 0, COLS, to=0),
          Chunk("q_up", "mla_w_q_up", "cT", 2, COLS, MLA_H * QK_D - COLS, to=COLS)]
    c += [Chunk("kv_up", "mla_w_kv_up", "kvT", 1, x, COLS, to=x // 128) for x in (0, COLS)]

    def gate(g):
        return [Chunk("gate", "w_in", "xT", KD, x, COLS, to=x) for x in (g, g + COLS)]

    def branch(n):
        return [Chunk("branch_" + n, "w_branch_" + n, "oT", 4, x, COLS, to=x) for x in (0, COLS)]

    c += gate(G_MLA) + gate(G_RET) + branch("mla") + gate(G_MOBA) + branch("ret") + branch("moba")
    c += [Chunk("residual", "w_out", "xT", KD, x, COLS, to=x) for x in (0, COLS)]
    c += [Chunk("up", "w_mlp_up", "xT", KD, x, COLS, to=4 * (x // COLS)) for x in range(0, D_FF, COLS)]
    c += [Chunk("residual_wide", "w_mlp_down", "hT", D_FF // P, 0, D, wide=True)]
    return c


def chunks_second():
    def p(first, end, n=COLS, to=None):
        return [Chunk("p", "w_in_2", "xT", KD, x, n, to=at2(x) if to is None else to) for x in range(first, end, n)]

    c = p(GQ, GV) + p(RA_F, AQ, 2 * GLA_R, RA) + p(GV, RA_F) + p(AQ, G_A)
    c += [Chunk("gate", "w_in_2", "xT", KD, x, COLS, to=at2(x)) for x in range(G_A, IN2_COLS, COLS)]
    c += [Chunk("branch_gla", "w_o_gla_2", "xT", KD, x, COLS, to=x) for x in (0, COLS)]
    c += [Chunk("branch_attn", "w_o_attn_2", "xT", KD, x, COLS, to=x) for x in (0, COLS)]
    c += [Chunk("normed", "w_out_2", "xT", KD, x, COLS, to=x) for x in (0, COLS)]
    for x in range(0, FFN, COLS):
        n = min(COLS, FFN - x)
        c += [Chunk("glu_gate", "w_ffn_in_2", "xT", KD, x, n, to=x // P), Chunk("glu_up", "w_ffn_in_2", "xT", KD, FFN + x, n, to=x // P)]
    c += [Chunk("normed_wide", "w_ffn_out_2", "hT", FFN // P, 0, D, wide=True)]
    c += [Chunk("plain_wide", "w_ple_proj_2", "pT", PLE // P, 0, D, wide=True)]
    c += [Chunk("ple", "w_ple_gate_2", "xT", KD, x, COLS, to=x) for x in (0, COLS)]
    return c


SIGNALS = {
    'unit_used'         : [140, 0, 160],
    'hi_ready'          : [140, 0, 160],
    'lo_ready'          : [140, 0, 160],
    'rows_ready'        : [20, 0, 24],
    'prob_ready'        : [16, 0, 0],
    'half_ready'        : [36, 0, 36],
    'variance'          : [4, 1, 7],
    'root_ready'        : [4, 1, 7],
    'norm_open'         : [4, 2, 6],
    'squares_done'      : [4, 2, 14],
    'logarithm'         : [4, 1, 9],
    'shift_ready'       : [16, 0, 8],
    'silu_ready'        : [1, 0, 1],
    'gates_ready'       : [2, 0, 1],
    'rotated'           : [1, 0, 0],
    'dve_step'          : [50, 8, 87],
    'params_free'       : [1, 0, 1],
    'params_loaded'     : [4, 0, 4],
    'step_open'         : [17, 0, 0],
    'x_final'           : [0, 1, 0],
    'minus_abs'         : [0, 0, 2],
    'softplus'          : [0, 0, 2],
    'walpha_used'       : [0, 0, 1],
    'walpha_loaded'     : [0, 0, 1],
    'states_ready'      : [0, 0, 4],
    'gg_ready'          : [0, 0, 1],
    'heads_done'        : [0, 0, 1],
    'pe_rows_loaded'    : [0, 0, 1],
    'glu_ready'         : [0, 0, 6],
    'bank0_drained'     : [25, 0, 27],
    'bank0_filled'      : [25, 0, 27],
    'bank1_drained'     : [27, 0, 28],
    'bank1_filled'      : [27, 0, 28],
    'bank2_drained'     : [22, 0, 27],
    'bank2_filled'      : [22, 0, 27],
    'bank3_drained'     : [18, 0, 26],
    'bank3_filled'      : [18, 0, 26],
    'gain0_free'        : [1, 0, 2],
    'gain0_loaded'      : [1, 0, 2],
    'gain1_free'        : [1, 0, 2],
    'gain1_loaded'      : [1, 0, 2],
    'gain2_free'        : [0, 1, 1],
    'gain2_loaded'      : [0, 1, 1],
    'pair0_drained'     : [18, 0, 19],
    'pair1_drained'     : [17, 0, 19],
    'raw0_loaded'       : [35, 0, 40],
    'raw1_loaded'       : [35, 0, 40],
    'raw2_loaded'       : [35, 0, 40],
    'raw3_loaded'       : [35, 0, 40],
}


FIRST, BETWEEN, SECOND = 0, 1, 2
REPEATS = [LAYERS, 1, LAYERS]


class Plan:

    def __init__(self, chunks):
        self.chunks = chunks
        self.unit = []
        uses = [0, 0]
        weights = set()
        turn = 0
        for i, c in enumerate(chunks):
            c.first = len(self.unit)
            self.unit += [(i, n) for n in range(c.units)]
            c.last = len(self.unit) - 1
            c.fresh = c.weight not in weights
            weights.add(c.weight)
            c.pairs = [0, 1] if c.wide else [turn % 2]
            turn += 0 if c.wide else 1
            c.use = [uses[x] for x in c.pairs]
            for x in c.pairs:
                uses[x] += 1
        self.n = len(self.unit)
        assert self.n % RING == 0
        self.ends = {c.last: c for c in chunks}

    def ended(self, u, after, before):
        return self.ends.get(u) if after <= u < before else None


class Stream:

    def __init__(self, plan, unit, follow):
        self.plan, self.unit, self.follow, self.u, self.after = plan, unit, follow, 0, 0

    def run(self, count):
        for _ in range(count):
            self.unit(self.u)
            self.trail(self.u)
            self.u += 1

    def trail(self, u):
        for delay, step in self.follow:
            c = self.plan.ended(u - delay, self.after, self.u + 1 if u == self.u else self.u)
            if c is not None:
                step(c)

    def finish(self):
        for u in range(self.u, self.u + 1 + max(d for d, _ in self.follow)):
            self.trail(u)
        self.after = self.u


class Counts:

    def __init__(self, sems, totals, credit, sent):
        self.sems, self.totals, self.credit, self.sent = sems, totals, credit, sent
        self.segment, self.layer, self.seen, self.own = 0, 0, {}, {}

    def enter(self, segment, Ler):
        self.segment, self.layer, self.seen, self.own = segment, Ler, {}, {}

    def at(self, name, n):
        t = self.totals[name]
        before = sum(t[s] * REPEATS[s] for s in range(self.segment))
        return self.sems[name], self.layer * t[self.segment] + (before + n + self.credit.get(name, 0))

    def dma(self, name, n):
        sem, value = self.at(name, n)
        return sem, value * 16

    def next(self, name, n=1):
        self.seen[name] = self.seen.get(name, 0) + n
        return self.at(name, self.seen[name])

    def up(self, name):
        self.own[name] = self.own.get(name, 0) + 1
        self.sent[name][self.segment] += 1
        return self.sems[name], 1


ONCE = ["x_loaded", "const_loaded", "ring_clear", "result_ready", "stored"]
CREDIT = {"pair0_drained": 1, "pair1_drained": 1, "lo_ready": 4, "unit_used": 4,
          **{f"bank{b}_drained": 1 for b in range(4)}, **{f"gain{s}_free": 1 for s in range(3)}, "params_free": 1, "walpha_used": 1}
GAIN_SLOT = {FIRST: [0, 1], BETWEEN: [2], SECOND: [0, 1, 0, 1, 2]}
EVAC, TURN = 1, 3


def spread(ap, axis, count):
    shape = list(ap.shape)
    return ap.unsqueeze(axis).broadcast_to(shape[:axis] + [count] + shape[axis:])


BY_TILE = ("w_in", "w_out", "w_mlp_up", "w_in_2", "w_o_gla_2", "w_o_attn_2", "w_out_2", "w_ffn_in_2", "w_ple_gate_2")


class Banks:

    def __init__(self):
        self.given, self.uses, self.turn = {}, [0] * 4, 0

    def get(self, key, among=(0, 1, 2, 3)):
        if key not in self.given:
            b = among[self.turn % len(among)]
            self.turn += 1
            self.given[key] = (b, self.uses[b])
            self.uses[b] += 1
        return self.given[key]


class Layout:
    pass


def build(nc, io, totals, sent):
    ctx = ExitStack()
    with ctx:
        def sb(name, shape, dt=F32):
            return ctx.enter_context(nc.sbuf_tensor(name, shape, dt))

        raw = sb("raw", [P, RING, 2, COLS])
        hi = sb("hi", [P, RING, 2, COLS], F32R)
        lo = sb("lo", [P, RING, 2, COLS], F32R)
        x = sb("x", [P, NT, D])
        y = sb("y", [P, NT, D])
        xT = [sb(f"xT{i}", [P, KD, TOK], F32R) for i in "hl"]
        gains = sb("gains", [P, 3, D])
        params = sb("params", [P, 1536])
        const = sb("const", [P, max(CONST_COLS)])
        small = sb("small", [P, 256])
        tmp = sb("tmp", [P, 1024])
        big = nc.sbuf_usable_end // 32 * 32 - 2 * 32 * TOK * 4
        hT = [nc.alloc_sbuf_tensor_at(f"hT{i}", [P, 32, TOK], F32R, offset=big + n * 32 * TOK * 4)
              for n, i in enumerate("hl")]
        proj = nc.alloc_sbuf_tensor_at("proj", [P, NT, IN2_COLS], F32, offset=big)
        spare = big + NT * IN2_COLS * 4
        arena = big - 30 * 1024
        assert nc.sbuf_base <= arena and spare + 10240 <= nc.sbuf_usable_end, (nc.sbuf_base, arena)

        def at(name, kib, shape, dt=F32, base=arena):
            return nc.alloc_sbuf_tensor_at(name, shape, dt, offset=base + int(kib * 1024))

        qT = at("qT", 0, [P, 8, TOK])
        kT = at("kT", 8, [P, 8, TOK])
        prob = at("prob", 16, [P, 2, 384])
        probT = at("probT", 19, [P, 2, 384])
        oT = [at("oTh", 22, [P, 4, TOK], F32R), at("oTl", 26, [P, 4, TOK], F32R)]
        km = at("km", 0, [P, NT, MLA_H, QK_D], base=spare)
        vm = at("vm", 6, [P, NT, MLA_H, MLA_V], base=spare)

        states = at("states", 16, [P, 2, 3, GLA_V])
        raT = at("raT", 16, [GLA_R, 2, TOK])
        qd = at("qd", 22, [P, NT, COLS])
        kd = at("kd", 26, [P, NT, COLS])
        seenT = at("seenT", 22, [P, 2, 2, NT, P])
        ks = at("ks", 0, [P, 2, NT, COLS], base=spare)
        silu = at("silu", 0, [P, NT, D], base=spare)
        wide = at("wide", 0, [P, 4 * D])
        attn = at("attn", 16, [P, 2, NT, TOK])
        attnT = at("attnT", 22, [P, 2, 4, P])
        pe_rows = at("pe_rows", 16, [P, NT, PLE])

        acc = ctx.enter_context(nc.psum_tensor("acc", [P, 4, COLS], F32))
        mix = ctx.enter_context(nc.psum_tensor("mix", [P, 4, COLS], F32))

        def cst(name, *shape):
            a, w = CONST_AT[name]
            v = const[:, a:a + w]
            if len(shape) == 2:
                v = v.rearrange("p (a b) -> p a b", a=shape[0])
            return v

        def normed(t):
            return acc[:, t:t + 3:2, :]

        ident = cst("ident")
        sems = {name: ctx.enter_context(nc.semaphore(name)) for name in [*totals, *ONCE]}
        plans = {FIRST: Plan(chunks_first()), SECOND: Plan(chunks_second())}
        banks = {s: Banks() for s in (FIRST, BETWEEN, SECOND)}
        acts = {"xT": xT, "hT": hT, "oT": oT, "cT": oT, "kvT": [a[:, 2:3] for a in oT], "pT": oT}
        L = Layout()
        L.normed = normed
        L.acc, L.acts, L.attn, L.attnT, L.banks, L.const, L.cst, L.gains = acc, acts, attn, attnT, banks, const, cst, gains
        L.hT, L.hi, L.ident, L.kT, L.kd, L.km, L.ks, L.lo = hT, hi, ident, kT, kd, km, ks, lo
        L.mix, L.oT, L.params, L.pe_rows, L.plans, L.prob, L.probT, L.proj = mix, oT, params, pe_rows, plans, prob, probT, proj
        L.qT, L.qd, L.raT, L.raw, L.seenT, L.sems, L.silu, L.small = qT, qd, raT, raw, seenT, sems, silu, small
        L.states, L.tmp, L.vm, L.wide, L.x, L.xT, L.y = states, tmp, vm, wide, x, xT, y
        block = ctx.enter_context(nc.Block())

        def counts():
            return Counts(sems, totals, CREDIT, sent)

        @block.tensor
        def _(pe):
            tensor_program(nc, pe, counts(), L)

        @block.sync
        def _(sp):
            sync_program(nc, sp, counts(), L, io)

        @block.gpsimd
        def _(pool):
            gpsimd_program(nc, pool, counts(), L)

        @block.scalar
        def _(act):
            scalar_program(nc, act, counts(), L, io)

        @block.vector
        def _(dve):
            vector_program(nc, dve, counts(), L)


KV_BANKS = (((0, 0), (0, 2)), ((0, 1), (1, 3)), ((1, 2),), ((1, 1),))
LAST_INTER = ((0, 2), (1, 2))


def tensor_program(nc, pe, n, L):
    seg = FIRST

    def fill(key, products, among=(0, 1, 2, 3)):
        b, use = L.banks[seg].get(key, among)
        pe.wait_ge(*n.at(f"bank{b}_drained", use))
        for last in products(b):
            pass
        last.then_inc(*n.up(f"bank{b}_filled"))

    def emptied(key):
        b, use = L.banks[seg].get(key)
        pe.wait_ge(*n.at(f"bank{b}_drained", use + 1))

    def turn(key, rows, tiles, width=P, among=(0, 1, 2, 3)):
        def products(b):
            for i, k in enumerate(tiles):
                for t in range(NT):
                    yield nc.tensor.transpose(L.mix[0:width, b, i * TOK + t * P:i * TOK + (t + 1) * P], rows(t, k), L.ident)
        fill(key, products, among)

    def turn_all(weight, rows, k_tiles):
        if weight in BY_TILE:
            for t in range(NT):
                pe.wait_ge(*n.next("rows_ready"))
                for g in range(0, k_tiles, 4):
                    fill((weight, t, g // 4), lambda b: [nc.tensor.transpose(L.mix[:, b, i * P:(i + 1) * P], rows(t, g + i), L.ident) for i in range(4)])
            return
        pe.wait_ge(*n.next("rows_ready"))
        for j in range(0, k_tiles, 2):
            turn((weight, j // 2), rows, range(j, min(j + 2, k_tiles)))

    def unit(u):
        plan = L.plans[seg]
        ci, j = plan.unit[u]
        c = plan.chunks[ci]
        slot = u % RING
        if j == 0:
            for pair, use in zip(c.pairs, c.use):
                pe.wait_ge(*n.at(f"pair{pair}_drained", use))
        if c.fresh and (not c.wide or j % 2 == 0):
            for key in [(c.weight, t, j // 2) for t in range(NT)] if c.weight in BY_TILE else [(c.weight, j // 2 if c.wide else j)]:
                emptied(key)
        pe.wait_ge(*n.at("hi_ready", u + 1))
        pe.wait_ge(*n.at("lo_ready", u + 1))
        ah, al = L.acts[c.act]
        for part in range(2 if c.wide or c.k_tiles > 1 else 1):
            k = j if c.wide else 2 * j + part
            for t in range(NT):
                out = L.acc[:, (2 * part if c.wide else 2 * c.pairs[0]) + t, 0:c.n if not c.wide else COLS]
                for a, w in ((ah, L.hi), (ah, L.lo), (al, L.hi)):
                    last = nc.tensor.matmul(out, a[:, k, t * P:(t + 1) * P], w[:, slot, part, 0:out.shape[1]],
                                            start=(k == 0 and a is ah and w is L.hi),
                                            stop=(k == c.k_tiles - 1 and a is al))
        last.then_inc(*n.up("unit_used"))

    def scores(tag, h, q, k):
        def products(b):
            for a, w, c in ((P, TOK, 0), (0, P, TOK)):
                yield nc.tensor.matmul(L.mix[:, b, c:c + w], q[:, a:a + P], k[:, 0:w], start=True, stop=True)
        fill((tag, "s", h), products, (0, 1, 2))

    def prob_turn(tag, h):
        pe.wait_ge(*n.next("prob_ready"))
        def products(b):
            for i in range(3):
                yield nc.tensor.transpose(L.mix[:, b, i * P:(i + 1) * P], L.prob[:, h % 2, i * P:(i + 1) * P], L.ident)
        fill((tag, "t", h), products, (0, 1, 2))

    def context(tag, h, v, dv, blocks, per):
        g, i = h // per, h % per
        b, use = L.banks[seg].get((tag, "o", g), (3,))
        if i == 0:
            pe.wait_ge(*n.at(f"bank{b}_drained", use))
        for t in range(NT):
            for kt in range(t + 1):
                c = blocks[t, kt]
                last = nc.tensor.matmul(L.mix[:, b, (t * per + i) * dv:(t * per + i + 1) * dv],
                                        L.probT[:, h % 2, c:c + P], v(kt, h), start=(kt == 0), stop=(kt == t))
        if i == per - 1:
            last.then_inc(*n.up(f"bank{b}_filled"))

    def softmax_heads(tag, heads, q, k, v, s, units):
        blocks = {(1, 0): 0, (1, 1): P, (0, 0): TOK}
        for h in range(heads + 2):
            if h < heads:
                scores(tag, h, q(h), k(h))
            if h >= 2:
                emptied((tag, "t", h - 2))
                context(tag, h - 2, v, MLA_V, blocks, 4)
            s.run(units[h] if h < len(units) else 0)
            if 1 <= h <= heads:
                prob_turn(tag, h - 1)

    def hidden_turn(c):
        if c.name == "up" or c.name == "glu_up":
            weight = "w_mlp_down" if c.name == "up" else "w_ffn_out_2"
            pe.wait_ge(*n.next("rows_ready"))
            slot = (c.to // 4) % 2
            for j in range(0, c.n // P, 2):
                turn((weight, (c.to + j) // 2), lambda t, k: L.y[:, t, slot * COLS + k * P:slot * COLS + (k + 1) * P], range(j, j + 2))

    def first_layer():
        s = Stream(L.plans[FIRST], unit, [(TURN, hidden_turn)])
        x_rows = lambda t, k: L.y[:, t, k * P:(k + 1) * P]
        turn_all("w_in", x_rows, KD)
        s.run(10)
        pe.wait_ge(*n.next("rows_ready"))
        latent = lambda t, k: L.proj[:, t, k * P:(k + 1) * P]
        turn(("mla_w_q_up", 0), latent, (0, 1))
        turn(("mla_w_kv_up", 0), latent, (2,))
        s.run(24 - 6 + 4 + 2)
        pe.wait_ge(*n.next("rows_ready"))
        for j in range(4):
            turn(("mla", "q", j), lambda t, h: L.y[:, t, h * QK_D:(h + 1) * QK_D], (2 * j, 2 * j + 1), QK_D)
        for j in range(4):
            turn(("mla", "k", j), lambda t, h: L.km[:, t, h, :], (2 * j, 2 * j + 1), QK_D)
        for j in range(4):
            emptied(("mla", "q", j)); emptied(("mla", "k", j))
        softmax_heads("mla", MLA_H, lambda h: L.qT[0:QK_D, h, :], lambda h: L.kT[0:QK_D, h, :],
                      lambda t, h: L.vm[:, t, h, :], s, [2, 2, 1, 2, 1, 2, 1, 2, 1, 0])
        pe.wait_ge(*n.next("rows_ready"))
        for w, col in (("q", RQ), ("k", RK)):
            turn(("ret", w, 0), lambda t, k: L.proj[:, t, col + k * P:col + (k + 1) * P], (0, 1))
        turn_all("w_branch_mla", x_rows, 4)
        emptied(("ret", "q", 0)); emptied(("ret", "k", 0))
        for h in range(RET_H + 1):
            if h < RET_H:
                lo_p = RET_K * (h % 2)
                q, k = (a[lo_p:lo_p + RET_K, h // 2, :] for a in (L.qT, L.kT))
                def products(b, q=q, k=k):
                    for kt, w, c in ((0, TOK, 0), (1, P, TOK)):
                        yield nc.tensor.matmul(L.mix[:, b, c:c + w], k[:, kt * P:(kt + 1) * P], q[:, kt * P:TOK], start=True, stop=True)
                fill(("ret", "s", h), products, (0, 1, 2))
            s.run(1 if h else 0)
            if h:
                emptied(("ret", "s", h - 1))
                context("ret", h - 1, lambda t, hh: L.proj[:, t, RV + hh * RET_V:RV + (hh + 1) * RET_V], RET_V,
                        {(0, 0): 0, (1, 0): P, (1, 1): TOK}, 2)
        for w, col in (("q", MQ), ("k", MK)):
            for j in range(2):
                turn(("moba", w, j), lambda t, k: L.proj[:, t, col + k * P:col + (k + 1) * P], (2 * j, 2 * j + 1))
        for w in "qk":
            for j in range(2):
                emptied(("moba", w, j))
        half = lambda a, h: a[MOBA_D * (h % 2):MOBA_D * (h % 2 + 1), h // 2, :]
        heads = lambda units: softmax_heads("moba", MOBA_H, lambda h: half(L.qT, h), lambda h: half(L.kT, h),
                      lambda t, h: L.proj[:, t, MV + h * MOBA_D:MV + (h + 1) * MOBA_D], s, units)
        heads([1, 1, 1, 1, 1, 1, 1, 1, 0, 0])
        turn_all("w_branch_ret", lambda t, k: L.y[:, t, COLS + k * P:COLS + (k + 1) * P], 4)
        s.run(4)
        turn_all("w_branch_moba", x_rows, 4)
        s.run(4)
        turn_all("w_out", lambda t, k: L.proj[:, t, G_MLA + k * P:G_MLA + (k + 1) * P], KD)
        s.run(8)
        turn_all("w_mlp_up", x_rows, KD)
        s.run(32)
        s.finish()
        s.run(32)
        assert s.u == L.plans[FIRST].n

    def second_layer():
        s = Stream(L.plans[SECOND], unit, [(TURN, hidden_turn)])
        y_rows = lambda t, k: L.y[:, t, k * P:(k + 1) * P]
        f32 = dict(start=True, stop=True)
        turn_all("w_in_2", y_rows, KD)
        s.run(14)
        pe.wait_ge(*n.next("rows_ready"))
        def ra_blocks(b):
            for d in range(2):
                for t in range(NT):
                    yield nc.tensor.transpose(L.mix[0:GLA_R, b, d * TOK + t * P:d * TOK + (t + 1) * P],
                                              L.proj[:, t, RA + d * GLA_R:RA + (d + 1) * GLA_R], L.ident)
        fill(("gla", "ra"), ra_blocks)
        s.run(2)
        for d in range(2):
            if d == 0:
                emptied(("gla", "ra"))
                pe.wait_ge(*n.dma("walpha_loaded", 1))
            for t in range(NT):
                fill(("gla", "z", d, t), lambda b: [nc.tensor.matmul(L.mix[:, b, :], L.raT[:, d, t * P:(t + 1) * P],
                                                                    L.tmp[0:GLA_R, d * COLS:(d + 1) * COLS], **f32)])
            s.run(2)
            pe.wait_ge(*n.next("rows_ready"))
            for t in range(NT):
                for what in ("cum", "rest"):
                    fill(("gla", what, d, t), lambda b: [nc.tensor.matmul(L.mix[:, b, :], L.cst(f"{what}_{'fb'[d]}"),
                                                                         L.y[:, t, 0:COLS], **f32)])
            def chunk_sums(b):
                for h in range(GLA_H):
                    for t in range(NT):
                        yield nc.tensor.matmul(L.mix[:, b, 4 * h + 2 * t:4 * h + 2 * t + 2], L.y[:, t, h * P:(h + 1) * P], L.cst("halves"), **f32)
            fill(("gla", "last", d), chunk_sums)
            s.run(3)
            pe.wait_ge(*n.next("rows_ready"))
            for w, rows in (("q", L.qd), ("k", L.kd)):
                for j in range(2):
                    turn(("gla", w, d, j), lambda t, h: rows[:, t, h * P:(h + 1) * P], (2 * j, 2 * j + 1))
            s.run(2)
        for d in range(2):
            for j in range(2):
                emptied(("gla", "q", d, j)); emptied(("gla", "k", d, j))

        def gla_head(h):
            gv = lambda r, t: L.proj[r, t, at2(GV) + h * GLA_V:at2(GV) + (h + 1) * GLA_V]
            def seen(b):
                for d in range(2):
                    for t in range(NT):
                        yield nc.tensor.matmul(L.mix[:, b, d * TOK + t * P:d * TOK + (t + 1) * P],
                                               L.kT[:, 4 * d + h, t * P:(t + 1) * P], L.qT[:, 4 * d + h, t * P:(t + 1) * P], **f32)
            fill(("gla", "s", h), seen)
            for i, pairs in enumerate(KV_BANKS):
                def kv(b):
                    for m, (d, c) in enumerate(pairs):
                        r = slice(GLA_CHUNK * (c % 2), GLA_CHUNK * (c % 2 + 1))
                        yield nc.tensor.matmul(L.mix[:, b, m * GLA_V:(m + 1) * GLA_V], L.ks[r, d, c // 2, h * P:(h + 1) * P], gv(r, c // 2), **f32)
                fill(("gla", "kv", h, i), kv)
            s.run(2)
            emptied(("gla", "s", h))
            pe.wait_ge(*n.next("states_ready"))
            def out(b):
                for t in range(NT):
                    o = L.mix[:, b, t * GLA_V:(t + 1) * GLA_V]
                    for d in range(2):
                        yield nc.tensor.matmul(o, L.seenT[:, h % 2, d, t, :], gv(slice(0, P), t), start=(d == 0), stop=False)
                    inter = [(c, d, i) for c in (2 * t, 2 * t + 1) for d, i in ((0, c - 1), (1, 2 - c)) if i >= 0]
                    for m, (c, d, i) in enumerate(inter):
                        r = GLA_CHUNK * (c % 2)
                        yield nc.tensor.matmul(o[r:r + GLA_CHUNK], L.qT[:, 4 * d + h, c * GLA_CHUNK:(c + 1) * GLA_CHUNK],
                                               L.states[:, d, i, :], start=False, stop=(m in LAST_INTER[t]))
            fill(("gla", "o", h), out)
            s.run(1)

        for h in range(GLA_H):
            gla_head(h)
        s.run(14)
        turn_all("w_o_gla_2", y_rows, KD)
        pe.wait_ge(*n.next("rows_ready"))
        for j in range(4):
            turn(("gqa", "q", j), lambda t, k: L.proj[:, t, at2(AQ) + k * P:at2(AQ) + (k + 1) * P], (2 * j, 2 * j + 1))
        turn(("gqa", "k", 0), lambda t, k: L.proj[:, t, at2(AK) + k * P:at2(AK) + (k + 1) * P], (0, 1))
        for j in range(4):
            emptied(("gqa", "q", j))
        emptied(("gqa", "k", 0))
        for h in range(AQ_H + 2):
            if h < AQ_H:
                kv = h // (AQ_H // AKV_H)
                fill(("gqa", "s", h), lambda b: [nc.tensor.matmul(L.mix[:, b, t * TOK:(t + 1) * TOK], L.qT[:, h, t * P:(t + 1) * P],
                                                                 L.kT[:, kv, :], **f32) for t in range(NT)], (0, 1, 2))
            if h >= 2:
                g, i, kv = (h - 2) // 2, h % 2, (h - 2) // (AQ_H // AKV_H)
                b, use = L.banks[seg].get(("gqa", "o", g), (3,))
                emptied(("gqa", "t", h - 2))
                if i == 0:
                    pe.wait_ge(*n.at(f"bank{b}_drained", use))
                for t in range(NT):
                    for kt in range(NT):
                        last = nc.tensor.matmul(L.mix[:, b, (2 * t + i) * P:(2 * t + i + 1) * P], L.attnT[:, h % 2, 2 * t + kt, :],
                                                L.proj[:, kt, at2(AV) + kv * P:at2(AV) + (kv + 1) * P], start=(kt == 0), stop=(kt == NT - 1))
                if i == 1:
                    last.then_inc(*n.up(f"bank{b}_filled"))
            s.run(1 if 1 <= h <= 8 else 0)
            if 1 <= h <= AQ_H:
                emptied(("gqa", "s", h - 1))
                fill(("gqa", "t", h - 1), lambda b: [nc.tensor.transpose(L.mix[:, b, (2 * t + kt) * P:(2 * t + kt + 1) * P],
                     L.attn[:, (h - 1) % 2, t, kt * P:(kt + 1) * P], L.ident) for t in range(NT) for kt in range(NT)], (0, 1, 2))
        turn_all("w_o_attn_2", y_rows, KD)
        s.run(8)
        turn_all("w_out_2", lambda t, k: L.proj[:, t, at2(G_A) + k * P:at2(G_A) + (k + 1) * P], KD)
        s.run(8)
        turn_all("w_ffn_in_2", y_rows, KD)
        s.run(48)
        s.finish()
        s.run(20)
        pe.wait_ge(*n.dma("pe_rows_loaded", 1))
        turn(("w_ple_proj_2", 0), lambda t, k: L.pe_rows[:, t, k * P:(k + 1) * P], (0, 1))
        s.run(4)
        turn_all("w_ple_gate_2", lambda t, k: L.x[:, t, k * P:(k + 1) * P], KD)
        s.run(8)
        assert s.u == L.plans[SECOND].n

    pe.sem_inc(L.sems["unit_used"], CREDIT["unit_used"])
    pe.wait_ge(L.sems["const_loaded"], 16)
    with pe.Fori(0, LAYERS) as layer:
        n.enter(FIRST, layer)
        first_layer()
    seg = SECOND
    pe.wait_ge(L.sems["const_loaded"], 32)
    with pe.Fori(0, LAYERS) as layer:
        n.enter(SECOND, layer)
        second_layer()


def sync_program(nc, sp, n, L, io):
    seg = FIRST

    def unit(u):
        plan = L.plans[seg]
        ci, j = plan.unit[u]
        c = plan.chunks[ci]
        slot = u % RING
        sp.wait_ge(*n.at("lo_ready", u - RING + 1))
        w = io[c.weight][n.layer]
        if c.wide:
            src, dst = w[j * P:(j + 1) * P, :], L.raw[:, slot].rearrange("p a b -> p (a b)")
        elif c.k_tiles == 1:
            src, dst = w[:, c.col:c.col + c.n], L.raw[:, slot, 0, 0:c.n]
        else:
            src = w[2 * j * P:(2 * j + 2) * P, c.col:c.col + c.n].rearrange("(k p) n -> p k n", p=P)
            dst = L.raw[:, slot, :, 0:c.n]
        sem, _ = n.up(f"raw{slot}_loaded")
        sp.dma_start(dst, src).then_inc(sem, 16)

    def gain(slot, row):
        sp.wait_ge(*n.at(f"gain{slot}_free", n.own.get(f"gain{slot}_loaded", 0)))
        sem, _ = n.up(f"gain{slot}_loaded")
        sp.dma_start(L.gains[:, slot], row.partition_broadcast(P)).then_inc(sem, 16)

    def narrow(parts):
        sp.wait_ge(*n.at("params_free", 0))
        col = 0
        for row in parts:
            sem, _ = n.up("params_loaded")
            sp.dma_start(L.params[:, col:col + row.shape[-1]], row.partition_broadcast(P)).then_inc(sem, 16)
            col += row.shape[-1]

    sp.wait_ge(L.sems["ring_clear"], 1)
    sp.dma_start(L.x[:, :, :], io["x"][0].rearrange("(t p) d -> p t d", p=P)).then_inc(L.sems["x_loaded"], 16)
    sp.dma_start(L.const[:, 0:CONST_COLS[0]], io["const_first"]).then_inc(L.sems["const_loaded"], 16)
    with sp.Fori(0, LAYERS) as layer:
        n.enter(FIRST, layer)
        gain(0, io["attn_norm"][layer])
        s = Stream(L.plans[FIRST], unit, [(0, lambda c: None)])
        s.run(4)
        narrow([io[w][layer] for w in ("mla_q_norm", "mla_kv_norm", "ret_gn_w", "ret_gn_b")])
        gain(1, io["mlp_norm"][layer])
        s.run(s.plan.n - 4)
    n.enter(BETWEEN, 0)
    gain(2, io["final_norm"])
    seg = SECOND
    with sp.Fori(0, LAYERS) as layer:
        n.enter(SECOND, layer)
        gain(0, io["g_mix_pre_2"][layer])
        s = Stream(L.plans[SECOND], unit, [(0, lambda c: None)])
        s.run(4)
        narrow([io["g_gla_out_2"][layer], io["g_q_norm_2"][layer], io["g_k_norm_2"][layer],
                io["b_alpha_2"][layer].rearrange("a b -> (a b)")])
        sp.wait_ge(*n.at("walpha_used", 0))
        sp.dma_start(L.tmp[0:GLA_R, :].rearrange("r (d c) -> r d c", d=2), io["w_alpha_up_2"][layer].rearrange("d r c -> r d c"))\
            .then_inc(n.up("walpha_loaded")[0], 16)
        gain(1, io["g_mix_post_2"][layer])
        s.run(20)
        gain(0, io["g_ffn_pre_2"][layer])
        gain(2, io["g_ple_post_2"][layer])
        s.run(80)
        gain(1, io["g_ffn_post_2"][layer])
        sp.wait_ge(*n.at("heads_done", 1))
        sp.dma_start(L.pe_rows[:, :, :], io["p_2"][layer, 0].rearrange("(t p) d -> p t d", p=P)).then_inc(n.up("pe_rows_loaded")[0], 16)
        s.run(s.plan.n - 104)
    sp.wait_ge(L.sems["result_ready"], 1)
    sp.dma_start(io["out"][0].rearrange("(t p) d -> p t d", p=P), L.x[:, :, :]).then_inc(L.sems["stored"], 16)
    sp.wait_ge(L.sems["stored"], 16)


def gpsimd_program(nc, pool, n, L):
    pool.sem_inc(L.sems["lo_ready"], CREDIT["lo_ready"])
    for seg in (FIRST, SECOND):
        rounds = L.plans[seg].n // RING * REPEATS[seg]
        n.enter(seg, 0)
        for _ in range(L.plans[seg].n):
            n.up("lo_ready")
        start = 0 if seg == FIRST else L.plans[FIRST].n // RING * LAYERS
        with pool.Fori(start, start + rounds) as r:
            for slot in range(RING):
                u = r * RING + slot
                pool.wait_ge(L.sems[f"raw{slot}_loaded"], r * 16 + 16)
                pool.wait_ge(L.sems["hi_ready"], u + 1)
                nc.gpsimd.tensor_tensor(L.lo[:, slot], L.raw[:, slot], L.hi[:, slot].bitcast(F32),
                                        ALU.subtract).then_inc(L.sems["lo_ready"], 1)


VAR, ROOT, NEWTON, MAXIMUM, SHIFT, SUMS, INVERSE, STATS, MOMENTS, PARTS = 0, 32, 64, 96, 100, 104, 120, 136, 184, 200
LASTS = 136
HALVES_AHEAD = 3


def scalar_program(nc, act, n, L, io):
    seg = FIRST

    def high(u):
        slot = u % RING
        act.wait_ge(*n.dma(f"raw{slot}_loaded", u // RING + 1))
        act.wait_ge(*n.at("unit_used", u - RING + 1))
        nc.scalar.activation(L.hi[:, slot], L.raw[:, slot], ACT.Copy).then_inc(*n.up("hi_ready"))

    def unit(u):
        if u + HALVES_AHEAD < L.plans[seg].n:
            high(u + HALVES_AHEAD)

    def filled(key):
        b, use = L.banks[seg].get(key)
        act.wait_ge(*n.at(f"bank{b}_filled", use + 1))
        return b

    def empty(key, dst, width, rows=P):
        b = filled(key)
        nc.scalar.activation(dst, L.mix[0:rows, b, 0:width], ACT.Copy).then_inc(*n.up(f"bank{b}_drained"))

    def halves(weight, first, k_tiles, dst, at=0):
        if weight in BY_TILE:
            for t in range(NT):
                for g in range(k_tiles // 4):
                    b = filled((weight, t, g))
                    nc.scalar.activation(dst[:, 4 * g:4 * g + 4, t * P:(t + 1) * P], L.mix[:, b, :].rearrange("p (k i) -> p k i", k=4), ACT.Copy)\
                        .then_inc(*n.up("half_ready"))
            return
        for j in range(0, k_tiles, 2):
            w = min(2, k_tiles - j)
            b = filled((weight, (first + j) // 2))
            nc.scalar.activation(dst[:, at + first + j:at + first + j + w, :], L.mix[:, b, 0:w * TOK], ACT.Copy).then_inc(*n.up("half_ready"))

    def root(width):
        act.wait_ge(*n.next("variance"))
        r = L.small[:, ROOT:ROOT + width]
        nc.scalar.activation(r, L.small[:, VAR:VAR + width], ACT.Ln).then_inc(*n.up("logarithm"))
        act.wait_ge(*n.next("logarithm"))
        nc.scalar.activation(r, r, ACT.Exp, scale=-0.5).then_inc(*n.up("root_ready"))

    def squares(src, scratch, half):
        act.wait_ge(*n.next("norm_open"))
        nc.scalar.activation(scratch, src, ACT.Square, scale=D ** -0.5, accum_out=L.small[:, PARTS + 2 * half:PARTS + 2 * half + 1])\
            .then_inc(*n.up("squares_done"))

    def squares_of_x(*halves):
        for half in halves:
            cols = slice(half * COLS, (half + 1) * COLS)
            squares(L.x[:, 0, cols], L.y[:, 0, cols], half)

    def softmax_exp(tag, h, scale):
        act.wait_ge(*n.next("shift_ready"))
        g, i, s = h // 4, h % 4, h % 2
        for t, c, w in ((1, 0, TOK), (0, TOK, P)):
            p = L.prob[:, s, c:c + w]
            last = nc.scalar.activation(p, p, ACT.Exp, bias=L.small[:, SHIFT + 2 * s + 1 - t:SHIFT + 2 * s + 2 - t], scale=scale,
                                 accum_out=L.small[:, SUMS + 8 * g + 4 * t + i:SUMS + 8 * g + 4 * t + i + 1])
        last.then_inc(*n.up("prob_ready"))

    def softmax_heads(tag, heads, scale, s, units, beside=None):
        for h in range(heads + 2):
            if h < heads:
                softmax_exp(tag, h, scale)
            if beside:
                beside(h)
            s.run(units[h] if h < len(units) else 0)
            if 1 <= h <= heads:
                empty((tag, "t", h - 1), L.probT[:, (h - 1) % 2, :], 384)

    def gate(c):
        if c.name == "gate":
            act.wait_ge(*n.at("unit_used", c.last + 1))
            p = c.pairs[0]
            nc.scalar.activation(L.proj[:, :, c.to:c.to + COLS], L.acc[:, 2 * p:2 * p + 2, :], ACT.Copy)\
                .then_inc(*n.up(f"pair{p}_drained"))
        elif c.name == "glu_gate":
            act.wait_ge(*n.at("unit_used", c.last + 1))
            p, slot = c.pairs[0], c.to // 4 % 2
            nc.scalar.activation(L.y[:, :, slot * COLS:slot * COLS + c.n], L.acc[:, 2 * p:2 * p + 2, 0:c.n], ACT.Sigmoid)\
                .then_inc(*n.up("glu_ready"))
        elif c.name == "ple":
            act.wait_ge(*n.at("unit_used", c.last + 1))
            p = c.pairs[0]
            nc.scalar.activation(L.proj[:, :, c.to:c.to + COLS], L.acc[:, 2 * p:2 * p + 2, :], ACT.Sigmoid)\
                .then_inc(*n.up(f"pair{p}_drained"))
            squares(L.y[:, 0, c.to:c.to + COLS], L.proj[:, 0, c.to:c.to + COLS], c.to // COLS)
        elif c.name == "residual":
            squares_of_x(c.to // COLS)
        elif c.name in ("normed", "normed_wide"):
            for half in range(2) if c.wide else (c.to // COLS,):
                act.wait_ge(*n.at("unit_used", c.last + 1))
                for t in range(NT):
                    nc.scalar.activation(L.proj[:, t, half * COLS:(half + 1) * COLS], L.acc[:, 2 * half + t, :], ACT.Square,
                                         scale=D ** -0.5, accum_out=L.small[:, PARTS + 2 * half + t:PARTS + 2 * half + t + 1])\
                        .then_inc(*n.up("squares_done"))

    def sigmoids(*cols):
        for c in L.plans[seg].chunks:
            if c.name == "gate" and any(g <= c.to < g + D for g in cols):
                act.wait_ge(*n.at(f"pair{c.pairs[0]}_drained", c.use[0] + 1))
        for g in cols:
            last = nc.scalar.activation(L.proj[:, :, g:g + D], L.proj[:, :, g:g + D], ACT.Sigmoid)
        last.then_inc(*n.up("gates_ready"))

    def hidden(c):
        if c.name == "up" or c.name == "glu_up":
            halves("w_mlp_down" if c.name == "up" else "w_ffn_out_2", c.to, c.n // P, L.hT[0])

    def first_layer():
        s = Stream(L.plans[FIRST], unit, [(EVAC, gate), (TURN, hidden)])
        for u in range(HALVES_AHEAD):
            high(u)
        squares_of_x(0, 1)
        root(2)
        halves("w_in", 0, KD, L.xT[0])
        s.run(10)
        root(4)
        halves("mla_w_q_up", 0, 2, L.oT[0])
        halves("mla_w_kv_up", 0, 1, L.oT[0], 2)
        s.run(24)
        for j in range(4):
            empty(("mla", "q", j), L.qT[0:QK_D, 2 * j:2 * j + 2, :], 2 * TOK, QK_D)
        softmax_heads("mla", MLA_H, QK_D ** -0.5, s, [2, 2, 1, 2, 1, 2, 1, 2, 1, 0])
        empty(("ret", "q", 0), L.qT[:, 0:2, :], 2 * TOK)
        halves("w_branch_mla", 0, 4, L.oT[0])
        s.run(1)
        act.wait_ge(*n.next("rotated"))
        nc.scalar.activation(L.tmp[:, :].rearrange("p (t c) -> p t c", t=NT), L.proj[:, :, RG:RG + COLS], ACT.Sigmoid)\
            .then_inc(*n.up("silu_ready"))
        sigmoids(G_MLA, G_RET)
        s.run(3)
        for j in range(2):
            empty(("moba", "q", j), L.qT[:, 2 * j:2 * j + 2, :], 2 * TOK)
        softmax_heads("moba", MOBA_H, MOBA_D ** -0.5, s, [1, 1, 1, 1, 1, 1, 1, 1, 0, 0],
                      lambda h: root(8) if h == 2 else None)
        halves("w_branch_ret", 0, 4, L.oT[0])
        s.run(1)
        sigmoids(G_MOBA)
        s.run(3)
        halves("w_branch_moba", 0, 4, L.oT[0])
        s.run(4)
        halves("w_out", 0, KD, L.xT[0])
        s.run(8)
        s.finish()
        root(2)
        halves("w_mlp_up", 0, KD, L.xT[0])
        s.run(32)
        s.finish()
        s.run(32)

    def second_layer():
        s = Stream(L.plans[SECOND], unit, [(EVAC, gate), (TURN, hidden)])
        for u in range(HALVES_AHEAD):
            high(u)
        squares_of_x(0, 1)
        root(2)
        halves("w_in_2", 0, KD, L.xT[0])
        s.run(14)
        empty(("gla", "ra"), L.raT[:, :, :], 2 * TOK, GLA_R)
        s.run(2)
        for d in range(2):
            s.run(2)
            act.wait_ge(*n.next("minus_abs"))
            e = L.y[:, :, COLS:2 * COLS]
            nc.scalar.activation(e, e, ACT.Exp).then_inc(*n.up("logarithm"))
            act.wait_ge(*n.next("logarithm"))
            nc.scalar.activation(e, e, ACT.Ln, bias=1.0).then_inc(*n.up("softplus"))
            for t in range(NT):
                b = filled(("gla", "cum", d, t))
                nc.scalar.activation(L.qd[:, t, :], L.mix[:, b, :], ACT.Exp)
                nc.scalar.activation(L.kd[:, t, :], L.mix[:, b, :], ACT.Exp, scale=-1.0).then_inc(*n.up(f"bank{b}_drained"))
                b = filled(("gla", "rest", d, t))
                nc.scalar.activation(L.ks[:, d, t, :], L.mix[:, b, :], ACT.Exp).then_inc(*n.up(f"bank{b}_drained"))
            b = filled(("gla", "last", d))
            nc.scalar.activation(L.small[:, LASTS + 16 * d:LASTS + 16 * d + 16], L.mix[:, b, 0:16], ACT.Exp).then_inc(*n.up(f"bank{b}_drained"))
            s.run(3)
            for j in range(2):
                empty(("gla", "q", d, j), L.qT[:, 4 * d + 2 * j:4 * d + 2 * j + 2, :], 2 * TOK)
            s.run(2)
        for h in range(GLA_H):
            s.run(2)
            empty(("gla", "o", h), L.y[:, :, h * GLA_V:(h + 1) * GLA_V], 2 * GLA_V)
            s.run(1)
        act.wait_ge(*n.next("gg_ready"))
        nc.scalar.activation(L.silu[:, :, :], L.proj[:, :, at2(GG):at2(GG) + D], ACT.Sigmoid).then_inc(*n.up("silu_ready"))
        root(8)
        s.run(8)
        root(NT * (AQ_H + AKV_H))
        s.run(6)
        halves("w_o_gla_2", 0, KD, L.xT[0])
        for j in range(4):
            empty(("gqa", "q", j), L.qT[:, 2 * j:2 * j + 2, :], 2 * TOK)
        for h in range(AQ_H + 2):
            if h < AQ_H:
                act.wait_ge(*n.next("shift_ready"))
                b, use = L.banks[seg].get(("gqa", "s", h))
                for t in range(NT):
                    last = nc.scalar.activation(L.attn[:, h % 2, t, :], L.mix[:, b, t * TOK:(t + 1) * TOK], ACT.Exp,
                                                bias=L.small[:, SHIFT + 2 * (h % 2) + t:SHIFT + 2 * (h % 2) + t + 1], scale=A_D ** -0.5,
                                                accum_out=L.small[:, SUMS + 4 * (h // 2) + 2 * t + h % 2:SUMS + 4 * (h // 2) + 2 * t + h % 2 + 1])
                last.then_inc(*n.up(f"bank{b}_drained"))
            s.run(1 if 1 <= h <= 8 else 0)
            if h == 1:
                sigmoids(at2(G_A), at2(G_B))
            if 1 <= h <= AQ_H:
                empty(("gqa", "t", h - 1), L.attnT[:, (h - 1) % 2, :, :], COLS)
        halves("w_o_attn_2", 0, KD, L.xT[0])
        s.run(8)
        halves("w_out_2", 0, KD, L.xT[0])
        s.run(8)
        s.finish()
        root(2)
        squares_of_x(0, 1)
        root(2)
        halves("w_ffn_in_2", 0, KD, L.xT[0])
        s.run(48)
        s.finish()
        s.run(20)
        halves("w_ple_proj_2", 0, 2, L.oT[0])
        s.run(2)
        s.finish()
        root(2)
        s.run(2)
        halves("w_ple_gate_2", 0, KD, L.xT[0])
        s.run(8)
        s.finish()
        root(2)

    with act.Fori(0, LAYERS) as layer:
        n.enter(FIRST, layer)
        first_layer()
    seg = BETWEEN
    n.enter(BETWEEN, 0)
    squares_of_x(0, 1)
    root(2)
    act.wait_ge(*n.next("x_final"))
    act.dma_start(L.const[:, 0:CONST_COLS[1]], io["const_second"]).then_inc(L.sems["const_loaded"], 16)
    seg = SECOND
    with act.Fori(0, LAYERS) as layer:
        n.enter(SECOND, layer)
        second_layer()


def vector_program(nc, dve, n, L):
    v = nc.vector
    seg = FIRST
    mix, small, proj, y, x = L.mix, L.small, L.proj, L.y, L.x

    def col(at, w=1):
        return small[:, at:at + w]

    def link(ins, name="dve_step"):
        ins.then_inc(*n.up(name))
        dve.wait_ge(*n.at(name, n.own[name]))

    def tell(name):
        dve.sem_inc(*n.up(name))

    def unit(u):
        pass

    def filled(key):
        b, use = L.banks[seg].get(key)
        dve.wait_ge(*n.at(f"bank{b}_filled", use + 1))
        return b

    def drain(ins, key):
        b, use = L.banks[seg].get(key)
        ins.then_inc(*n.up(f"bank{b}_drained"))
        dve.wait_ge(*n.at(f"bank{b}_drained", use + 1))

    def empty(key, dst, width, rows=P):
        b = filled(key)
        drain(v.tensor_copy(dst, mix[0:rows, b, 0:width]), key)

    def halves(weight, first, k_tiles, dst, at=0):
        if weight in BY_TILE:
            for t in range(NT):
                for g in range(k_tiles // 4):
                    b, use = L.banks[seg].get((weight, t, g))
                    dve.wait_ge(*n.next("half_ready"))
                    hi, lo = (a[:, 4 * g:4 * g + 4, t * P:(t + 1) * P] for a in dst)
                    v.tensor_tensor(lo, mix[:, b, :].rearrange("p (k i) -> p k i", k=4), hi.bitcast(F32), ALU.subtract)\
                        .then_inc(*n.up(f"bank{b}_drained"))
            return
        for j in range(0, k_tiles, 2):
            w = min(2, k_tiles - j)
            key = (weight, (first + j) // 2)
            b, use = L.banks[seg].get(key)
            dve.wait_ge(*n.next("half_ready"))
            at_j = slice(at + first + j, at + first + j + w)
            v.tensor_tensor(dst[1][:, at_j, :], mix[:, b, 0:w * TOK].rearrange("p (k t) -> p k t", k=w),
                            dst[0][:, at_j, :].bitcast(F32), ALU.subtract).then_inc(*n.up(f"bank{b}_drained"))

    def refine(width):
        dve.wait_ge(*n.next("root_ready"))
        va, r, a = col(VAR, width), col(ROOT, width), col(NEWTON, width)
        link(v.tensor_tensor(a, r, r, ALU.mult))
        link(v.scalar_tensor_tensor(out=a, in0=a, scalar=-0.5, in1=va, op0=ALU.mult, op1=ALU.mult))
        link(v.scalar_tensor_tensor(out=r, in0=a, scalar=1.5, in1=r, op0=ALU.add, op1=ALU.mult))

    def mean_square(scratch, rows, out):
        return v.tensor_tensor_reduce(out=scratch, in0=rows, in1=rows, scale=1.0 / rows.shape[-1], scalar=NORM_EPS, op0=ALU.mult, op1=ALU.add, accum_out=out)

    def squares(src, scratch, half):
        tell("norm_open")
        link(v.tensor_tensor_reduce(out=scratch, in0=src, in1=src, scale=1.0 / D, scalar=0.0, op0=ALU.mult, op1=ALU.add,
                                    accum_out=col(PARTS + 2 * half + 1)))

    def squares_of_x(*halves):
        for half in halves:
            cols = slice(half * COLS, (half + 1) * COLS)
            squares(x[:, 1, cols], y[:, 1, cols], half)

    def variance():
        link(v.scalar_tensor_tensor(out=col(VAR, NT), in0=col(PARTS, NT), scalar=NORM_EPS, in1=col(PARTS + NT, NT), op0=ALU.add, op1=ALU.add), "variance")

    def gain_landed(slot):
        dve.wait_ge(*n.dma(f"gain{slot}_loaded", n.own.get(f"gain{slot}_free", 0) + 1))

    def norm_rows(slot, dst, turned=True):
        dve.wait_ge(*n.next("squares_done", 2))
        variance()
        gain_landed(slot)
        link(v.tensor_tensor(dst[:, 0], x[:, 0], L.gains[:, slot], ALU.mult))
        refine(NT)
        link(v.tensor_scalar(dst[:, 0], dst[:, 0], col(ROOT), None, ALU.mult))
        if turned:
            tell("rows_ready")
        link(v.scalar_tensor_tensor(out=dst[:, 1], in0=x[:, 1], scalar=col(ROOT + 1), in1=L.gains[:, slot], op0=ALU.mult, op1=ALU.mult))
        if turned:
            tell("rows_ready")
        tell(f"gain{slot}_free")

    def product_times_gains(c):
        gain_landed(1)
        for i in range(len(c.pairs)):
            half = c.to // COLS + i
            cols = slice(half * COLS, (half + 1) * COLS)
            for t in range(NT):
                dve.wait_ge(*n.next("squares_done"))
                last = v.tensor_tensor(y[:, t, cols], pair(c, i)[:, t], L.gains[:, 1, cols], ALU.mult)
            drained(last, c, i)

    def norm_add(slot, scaled=False, turned=False):
        if not scaled:
            dve.wait_ge(*n.next("squares_done", 2))
        variance()
        if not scaled:
            gain_landed(slot)
            for t in range(NT):
                last = v.tensor_tensor(y[:, t], y[:, t], L.gains[:, slot], ALU.mult)
            link(last)
        tell(f"gain{slot}_free")
        refine(NT)
        for t in range(NT):
            link(v.scalar_tensor_tensor(out=x[:, t], in0=y[:, t], scalar=col(ROOT + t), in1=x[:, t], op0=ALU.mult, op1=ALU.add))
            if turned:
                tell("rows_ready")

    def rope(a, b, c, s, shape, scratch=None, apart=512):
        size = int(np.prod(shape))
        names = "xyz"[:len(shape)]
        pat = f"p ({' '.join(names)}) -> p {' '.join(names)}"
        scratch = L.tmp if scratch is None else scratch
        u1, u2 = (scratch[:, i * apart:i * apart + size].rearrange(pat, **dict(zip(names, shape))) for i in range(2))
        v.tensor_tensor(u1, b, s, ALU.mult)
        link(v.tensor_tensor(u2, a, s, ALU.mult))
        v.tensor_tensor(a, a, c, ALU.mult)
        link(v.tensor_tensor(b, b, c, ALU.mult))
        v.tensor_tensor(a, a, u1, ALU.subtract)
        link(v.tensor_tensor(b, b, u2, ALU.add))

    def rope_heads(rows, heads, half, table):
        c, s = (spread(L.cst(f"{k}_{table}", NT, half), 2, heads) for k in "cs")
        rope(rows[:, :, :, 0:half], rows[:, :, :, half:2 * half], c, s, [NT, heads, half])

    def softmax_shift(tag, h, scale):
        s = h % 2
        key = (tag, "s", h)
        b = filled(key)
        tell("step_open")
        for i, c, w in ((0, 0, TOK), (1, TOK, P)):
            last = v.tensor_tensor_reduce(out=L.prob[:, s, c:c + w], in0=mix[:, b, c:c + w], in1=L.cst("causal")[:, c:c + w],
                                   scale=1.0, scalar=-3e38, op0=ALU.add, op1=ALU.max, accum_out=col(MAXIMUM + 2 * s + i))
        drain(last, key)
        v.tensor_scalar(col(SHIFT + 2 * s, 2), col(MAXIMUM + 2 * s, 2), -scale, None, ALU.mult).then_inc(*n.up("shift_ready"))

    def softmax_out(tag, g, base):
        key = (tag, "o", g)
        b = filled(key)
        link(v.reciprocal(col(INVERSE, 8), col(SUMS + 8 * g, 8)))
        inv = spread(col(INVERSE, 8).rearrange("p (t h) -> p t h", t=NT), 3, 64)
        drain(v.tensor_tensor(y[:, :, base:base + 256].rearrange("p t (h d) -> p t h d", h=4),
                              mix[:, b, :].rearrange("p (t h d) -> p t h d", t=NT, h=4), inv, ALU.mult), key)

    def softmax_heads(tag, heads, scale, base, s, units, beside=None):
        for h in range(heads + 2):
            if h < heads:
                softmax_shift(tag, h, scale)
            if beside:
                beside(h)
            if h >= 2 and (h - 2) % 4 == 3:
                softmax_out(tag, (h - 2) // 4, base + (h - 2) // 4 * 256)
            s.run(units[h] if h < len(units) else 0)
        tell("rows_ready")

    def pair(c, i=0):
        return L.acc[:, 2 * c.pairs[i]:2 * c.pairs[i] + 2, :]

    def drained(ins, c, i=0):
        name = f"pair{c.pairs[i]}_drained"
        ins.then_inc(*n.up(name))
        dve.wait_ge(*n.at(name, c.use[i] + 1))

    def read_out(c):
        if c.name == "gate":
            return
        dve.wait_ge(*n.at("unit_used", c.last + 1))
        if c.name == "p":
            drained(v.tensor_copy(proj[:, :, c.to:c.to + c.n], pair(c)[:, :, 0:c.n]), c)
        elif c.name == "q_up":
            drained(v.tensor_copy(y[:, :, c.to:c.to + c.n], pair(c)[:, :, 0:c.n]), c)
        elif c.name == "kv_up":
            heads = pair(c).rearrange("p t (h d) -> p t h d", h=4)
            v.tensor_copy(L.km[:, :, c.to:c.to + 4, 0:NOPE], heads[:, :, :, 0:NOPE])
            drained(v.tensor_copy(L.vm[:, :, c.to:c.to + 4, :], heads[:, :, :, NOPE:]), c)
        elif c.name.startswith("branch"):
            if c.name in ("branch_mla", "branch_moba", "branch_gla") and c.col == 0:
                dve.wait_ge(*n.next("gates_ready"))
            g = {"branch_mla": G_MLA, "branch_ret": G_RET, "branch_moba": G_MOBA,
                 "branch_gla": at2(G_A), "branch_attn": at2(G_B)}[c.name] + c.to
            drained(v.tensor_tensor(proj[:, :, g:g + COLS], proj[:, :, g:g + COLS], pair(c), ALU.mult), c)
            if c.name not in ("branch_mla", "branch_gla"):
                into = (G_MLA if seg == FIRST else at2(G_A)) + c.to
                m = proj[:, :, into:into + COLS]
                link(v.tensor_tensor(m, m, proj[:, :, g:g + COLS], ALU.add))
        elif c.name.startswith("residual"):
            for i in range(len(c.pairs)):
                r = x[:, :, c.to + i * COLS:c.to + (i + 1) * COLS]
                drained(v.tensor_tensor(r, r, pair(c, i), ALU.add), c, i)
            if c.name == "residual":
                squares_of_x(c.to // COLS)
        elif c.name in ("normed", "normed_wide"):
            product_times_gains(c)
        elif c.name == "up":
            slot = (c.to // 4) % 2
            r = y[:, :, slot * COLS:(slot + 1) * COLS]
            drained(v.tensor_scalar(r, pair(c), 0.0, None, ALU.max), c)
            v.tensor_tensor(r, r, r, ALU.mult).then_inc(*n.up("rows_ready"))

        elif c.name == "plain_wide":
            for i in range(2):
                drained(v.tensor_copy(y[:, :, i * COLS:(i + 1) * COLS], pair(c, i)), c, i)
        elif c.name == "glu_gate":
            slot = c.to // 4 % 2
            r = y[:, :, slot * COLS:slot * COLS + c.n]
            dve.wait_ge(*n.next("glu_ready"))
            drained(v.tensor_tensor(r, r, pair(c)[:, :, 0:c.n], ALU.mult), c)
        elif c.name == "ple":
            dve.wait_ge(*n.at(f"pair{c.pairs[0]}_drained", c.use[0] + 1))
            r = y[:, :, c.to:c.to + COLS]
            link(v.tensor_tensor(r, r, proj[:, :, c.to:c.to + COLS], ALU.mult))
            squares(y[:, 1, c.to:c.to + COLS], proj[:, 1, c.to:c.to + COLS], c.to // COLS)
        elif c.name == "glu_up":
            slot = c.to // 4 % 2
            r = y[:, :, slot * COLS:slot * COLS + c.n]
            drained(v.tensor_tensor(r, r, pair(c)[:, :, 0:c.n], ALU.mult), c)
            tell("rows_ready")

    def hidden(c):
        if c.name == "up" or c.name == "glu_up":
            halves("w_mlp_down" if c.name == "up" else "w_ffn_out_2", c.to, c.n // P, L.hT)

    def retention_out(step):
        o = y[:, :, COLS:2 * COLS]
        oh = [(t, h, y[:, t, COLS + h * RET_V:COLS + (h + 1) * RET_V]) for t in range(NT) for h in range(RET_H)]
        gate = L.tmp[:, :].rearrange("p (t c) -> p t c", t=NT)
        if step == 0:
            for i, (t, h, r) in enumerate(oh):
                last = v.bn_stats(col(STATS + 6 * i, 6), r)
            link(last)
        elif step == 1:
            tell("step_open")
            for i in range(8):
                last = v.bn_aggr(col(MOMENTS + 2 * i, 2), col(STATS + 6 * i, 6))
            link(last)
            v.tensor_scalar(col(VAR, 8), small[:, MOMENTS + 1:MOMENTS + 16:2], GN_EPS, None, ALU.add).then_inc(*n.up("variance"))
        elif step == 2:
            dve.wait_ge(*n.next("silu_ready"))
            link(v.tensor_tensor(gate, gate, proj[:, :, RG:RG + COLS], ALU.mult))
        elif step == 3:
            refine(8)
            for i, (t, h, r) in enumerate(oh):
                last = v.tensor_scalar(r, r, col(MOMENTS + 2 * i), col(ROOT + i), ALU.subtract, ALU.mult)
            link(last)
        elif step in (4, 5):
            gain = spread(L.params[:, 384 + (step - 4) * COLS:384 + (step - 3) * COLS], 1, NT)
            link(v.tensor_tensor(o, o, gain, (ALU.mult, ALU.add)[step - 4]))
        elif step == 6:
            tell("params_free")
            link(v.tensor_tensor(o, o, gate, ALU.mult))
            tell("rows_ready")

    def first_layer():
        s = Stream(L.plans[FIRST], unit, [(EVAC, read_out), (TURN, hidden)])
        squares_of_x(0, 1)
        norm_rows(0, y)
        halves("w_in", 0, KD, L.xT)
        s.run(6)
        dve.wait_ge(*n.dma("params_loaded", 4))
        for i, (a, w) in enumerate(((CQ, MLA_Q), (CKV, MLA_KV))):
            for t in range(NT):
                last = mean_square(L.tmp[:, (2 * i + t) * 256:(2 * i + t) * 256 + w], proj[:, t, a:a + w], col(VAR + 2 * i + t))
        link(last)
        tell("variance")
        rope_heads(proj[:, :, KR:KR + ROPE].rearrange("p t (h d) -> p t h d", h=1), 1, ROPE // 2, "mla")
        s.run(4)
        refine(4)
        for i, (a, w, g) in enumerate(((CQ, MLA_Q, 0), (CKV, MLA_KV, MLA_Q))):
            for t in range(NT):
                r = proj[:, t, a:a + w]
                last = v.scalar_tensor_tensor(out=r, in0=r, scalar=col(ROOT + 2 * i + t), in1=L.params[:, g:g + w], op0=ALU.mult, op1=ALU.mult)
        last.then_inc(*n.up("rows_ready"))
        halves("mla_w_q_up", 0, 2, L.oT)
        halves("mla_w_kv_up", 0, 1, L.oT, 2)
        v.tensor_copy(L.km[:, :, :, NOPE:], spread(proj[:, :, KR:KR + ROPE], 2, MLA_H))
        s.run(20)
        rope_heads(proj[:, :, MQ:MV].rearrange("p t (h d) -> p t h d", d=MOBA_D), 2 * MOBA_H, MOBA_R // 2, "moba")
        s.run(3)
        s.run(1)
        rope_heads(y[:, :, 0:MLA_H * QK_D].rearrange("p t (h d) -> p t h d", d=QK_D)[:, :, :, NOPE:], MLA_H, ROPE // 2, "mla")
        tell("rows_ready")
        for j in range(4):
            empty(("mla", "k", j), L.kT[0:QK_D, 2 * j:2 * j + 2, :], 2 * TOK, QK_D)
        rope_heads(proj[:, :, RQ:RV].rearrange("p t (h d) -> p t h d", d=RET_K), 2 * RET_H, RET_K // 2, "ret")
        tell("rotated")
        softmax_heads("mla", MLA_H, QK_D ** -0.5, 0, s, [2, 2, 1, 2, 1, 2, 1, 2, 1, 0])
        tell("rows_ready")
        empty(("ret", "k", 0), L.kT[:, 0:2, :], 2 * TOK)
        halves("w_branch_mla", 0, 4, L.oT)
        for h in range(RET_H + 1):
            if h < RET_H:
                key = ("ret", "s", h)
                b = filled(key)
                drain(v.tensor_tensor(L.probT[:, h % 2, :], mix[:, b, 0:384], L.cst("decay", RET_H, 384)[:, h], ALU.mult), key)
            s.run(1 if h else 0)
            if h in (2, 4):
                g = h // 2 - 1
                key = ("ret", "o", g)
                b = filled(key)
                drain(v.tensor_copy(y[:, :, COLS + g * 256:COLS + (g + 1) * 256], mix[:, b, :].rearrange("p (t c) -> p t c", t=NT)), key)
        for j in range(2):
            empty(("moba", "k", j), L.kT[:, 2 * j:2 * j + 2, :], 2 * TOK)
        softmax_heads("moba", MOBA_H, MOBA_D ** -0.5, 0, s, [1, 1, 1, 1, 1, 1, 1, 1, 0, 0], retention_out)
        halves("w_branch_ret", 0, 4, L.oT)
        s.run(4)
        halves("w_branch_moba", 0, 4, L.oT)
        s.run(4)
        s.finish()
        tell("rows_ready"); tell("rows_ready")
        halves("w_out", 0, KD, L.xT)
        s.run(8)
        s.finish()
        norm_rows(1, y)
        halves("w_mlp_up", 0, KD, L.xT)
        s.run(32)
        s.finish()
        s.run(32)
        s.finish()

    def gla_states(h):
        for d in range(2):
            for i in range(3):
                c = i if d == 0 else 3 - i
                j = next(j for j, pairs in enumerate(KV_BANKS) if (d, c) in pairs)
                m = KV_BANKS[j].index((d, c))
                key = ("gla", "kv", h, j)
                b = filled(key)
                kv = mix[:, b, m * GLA_V:(m + 1) * GLA_V]
                if i == 0:
                    ins = v.tensor_copy(L.states[:, d, 0, :], kv)
                else:
                    ins = v.scalar_tensor_tensor(out=L.states[:, d, i, :], in0=L.states[:, d, i - 1, :],
                                                 scalar=col(LASTS + 16 * d + 4 * h + c), in1=kv, op0=ALU.mult, op1=ALU.add)
                if m == len(KV_BANKS[j]) - 1:
                    drain(ins, key)
                else:
                    link(ins)
        tell("states_ready")

    def second_layer():
        s = Stream(L.plans[SECOND], unit, [(EVAC, read_out), (TURN, hidden)])
        squares_of_x(0, 1)
        norm_rows(0, y)
        halves("w_in_2", 0, KD, L.xT)
        s.run(14)
        tell("rows_ready")
        s.run(2)
        dve.wait_ge(*n.dma("params_loaded", 4))
        la, e = y[:, :, 0:COLS], y[:, :, COLS:2 * COLS]
        for d in range(2):
            for t in range(NT):
                key = ("gla", "z", d, t)
                b = filled(key)
                bias = L.params[:, COLS * (d + 1):COLS * (d + 2)]
                drain(v.tensor_tensor(y[:, t, 0:COLS], mix[:, b, :], bias, ALU.add), key)
            if d == 1:
                tell("walpha_used")
            link(v.scalar_tensor_tensor(out=e, in0=la, scalar=-1.0, in1=la, op0=ALU.mult, op1=ALU.min))
            tell("minus_abs")
            link(v.tensor_scalar(la, la, 0.0, None, ALU.min))
            s.run(2)
            dve.wait_ge(*n.next("softplus"))
            link(v.tensor_tensor(la, la, e, ALU.subtract))
            tell("rows_ready")
            b, use = L.banks[seg].get(("gla", "last", d))
            dve.wait_ge(*n.at(f"bank{b}_drained", use + 1))
            gq, gk = proj[:, :, GQ:GQ + COLS], proj[:, :, GK:GK + COLS]
            v.scalar_tensor_tensor(out=L.qd[:, :, :], in0=L.qd[:, :, :], scalar=GLA_K ** -0.5, in1=gq, op0=ALU.mult, op1=ALU.mult)
            link(v.tensor_tensor(L.kd[:, :, :], L.kd[:, :, :], gk, ALU.mult))
            tell("rows_ready")
            link(v.tensor_tensor(L.ks[:, d], L.ks[:, d], gk, ALU.mult))
            s.run(3)
            for j in range(2):
                empty(("gla", "k", d, j), L.kT[:, 4 * d + 2 * j:4 * d + 2 * j + 2, :], 2 * TOK)
            s.run(2)
        for h in range(GLA_H):
            key = ("gla", "s", h)
            b = filled(key)
            for d in range(2):
                mask = spread(L.cst("in_" + "fb"[d]), 1, NT)
                last = v.tensor_tensor(L.seenT[:, h % 2, d], mix[:, b, d * TOK:(d + 1) * TOK].rearrange("p (t i) -> p t i", t=NT), mask, ALU.mult)
            drain(last, key)
            gla_states(h)
            s.run(2)
            s.run(1)
        tell("gg_ready")
        b, use = L.banks[seg].get(("gla", "o", GLA_H - 1))
        dve.wait_ge(*n.at(f"bank{b}_drained", use + 1))
        oh = [y[:, t, h * GLA_V:(h + 1) * GLA_V] for t in range(NT) for h in range(GLA_H)]
        for i, r in enumerate(oh):
            last = mean_square(L.wide[:, i * GLA_V:(i + 1) * GLA_V], r, col(VAR + i))
        link(last)
        tell("variance")
        refine(8)
        for i, r in enumerate(oh):
            last = v.scalar_tensor_tensor(out=r, in0=r, scalar=col(ROOT + i), in1=L.params[:, 0:GLA_V], op0=ALU.mult, op1=ALU.mult)
        link(last)
        dve.wait_ge(*n.next("silu_ready"))
        g = L.silu[:, :, :]
        link(v.tensor_tensor(g, g, proj[:, :, at2(GG):at2(GG) + D], ALU.mult))
        for t in range(NT):
            link(v.tensor_tensor(y[:, t], y[:, t], g[:, t], ALU.mult))
            tell("rows_ready")
        aqk = [proj[:, t, at2(AQ) + h * A_D:at2(AQ) + (h + 1) * A_D] for t in range(NT) for h in range(AQ_H + AKV_H)]
        for i, r in enumerate(aqk):
            last = mean_square(L.wide[:, i * A_D:(i + 1) * A_D], r, col(VAR + i))
        link(last)
        tell("variance")
        refine(20)
        for i, r in enumerate(aqk):
            w = 256 if i % 10 < AQ_H else 384
            last = v.scalar_tensor_tensor(out=r, in0=r, scalar=col(ROOT + i), in1=L.params[:, w:w + A_D], op0=ALU.mult, op1=ALU.mult)
        link(last)
        tell("params_free")
        for t in range(NT):
            r = proj[:, t, at2(AQ):at2(AV)].rearrange("p (h a s d) -> p h a s d", a=2, s=2, d=A_D // 4)
            c, sn = (spread(L.cst(f"{w}_ax", NT, 64)[:, t].rearrange("p (a d) -> p a d", a=2), 1, AQ_H + AKV_H) for w in "cs")
            rope(r[:, :, :, 0, :], r[:, :, :, 1, :], c, sn, [AQ_H + AKV_H, 2, A_D // 4], L.wide, 1024)
        s.run(14)
        tell("rows_ready")
        halves("w_o_gla_2", 0, KD, L.xT)
        empty(("gqa", "k", 0), L.kT[:, 0:2, :], 2 * TOK)
        for h in range(AQ_H + 2):
            if h < AQ_H:
                b = filled(("gqa", "s", h))
                m = 2 * (h % 2)
                link(v.tensor_reduce(col(MAXIMUM + m, 2), mix[:, b, :].rearrange("p (t k) -> p t k", t=NT), AX.X, ALU.max))
                v.tensor_scalar(col(SHIFT + m, 2), col(MAXIMUM + m, 2), -(A_D ** -0.5), None, ALU.mult).then_inc(*n.up("shift_ready"))
            if h >= 3 and h % 2 == 1:
                g = (h - 3) // 2
                key = ("gqa", "o", g)
                b = filled(key)
                link(v.reciprocal(col(INVERSE, 4), col(SUMS + 4 * g, 4)))
                inv = spread(col(INVERSE, 4).rearrange("p (t h) -> p t h", t=NT), 3, A_D)
                drain(v.tensor_tensor(y[:, :, g * 256:(g + 1) * 256].rearrange("p t (h d) -> p t h d", h=2),
                                      mix[:, b, :].rearrange("p (t h d) -> p t h d", t=NT, h=2), inv, ALU.mult), key)
            s.run(1 if 1 <= h <= 8 else 0)
        tell("rows_ready"); tell("rows_ready")
        tell("heads_done")
        halves("w_o_attn_2", 0, KD, L.xT)
        s.run(8)
        s.finish()
        tell("rows_ready"); tell("rows_ready")
        halves("w_out_2", 0, KD, L.xT)
        s.run(8)
        s.finish()
        norm_add(1, scaled=True)
        squares_of_x(0, 1)
        norm_rows(0, y)
        halves("w_ffn_in_2", 0, KD, L.xT)
        s.run(48)
        s.finish()
        s.run(20)
        halves("w_ple_proj_2", 0, 2, L.oT)
        s.run(2)
        s.finish()
        norm_add(1, scaled=True, turned=True)
        s.run(2)
        halves("w_ple_gate_2", 0, KD, L.xT)
        s.run(8)
        s.finish()
        norm_add(2)

    for b in range(4):
        dve.sem_inc(L.sems[f"bank{b}_drained"], 1)
    for name in ("pair0_drained", "pair1_drained", "gain0_free", "gain1_free", "gain2_free", "params_free"):
        dve.sem_inc(L.sems[name], 1)
    for slot in range(RING):
        last = v.memset(L.raw[:, slot], 0.0)
    last.then_inc(L.sems["ring_clear"], 1)
    dve.wait_ge(L.sems["x_loaded"], 16)
    dve.wait_ge(L.sems["const_loaded"], 16)
    with dve.Fori(0, LAYERS) as layer:
        n.enter(FIRST, layer)
        first_layer()
    seg = BETWEEN
    n.enter(BETWEEN, 0)
    squares_of_x(0, 1)
    norm_rows(2, x, turned=False)
    tell("x_final")
    dve.sem_inc(L.sems["walpha_used"], 1)
    seg = SECOND
    dve.wait_ge(L.sems["const_loaded"], 32)
    with dve.Fori(0, LAYERS) as layer:
        n.enter(SECOND, layer)
        second_layer()
    dve.sem_inc(L.sems["result_ready"], 1)



INPUTS = ['x', 'attn_norm', 'w_in', 'mla_q_norm', 'mla_kv_norm', 'mla_w_q_up', 'mla_w_kv_up', 'ret_gn_w', 'ret_gn_b',
 'w_branch_mla', 'w_branch_moba', 'w_branch_ret', 'w_out', 'mlp_norm', 'w_mlp_up', 'w_mlp_down', 'final_norm',
 'p_2', 'g_mix_pre_2', 'w_in_2', 'w_alpha_up_2', 'b_alpha_2', 'g_gla_out_2', 'g_q_norm_2', 'g_k_norm_2',
 'w_o_gla_2', 'w_o_attn_2', 'w_out_2', 'g_mix_post_2', 'g_ffn_pre_2', 'w_ffn_in_2', 'w_ffn_out_2',
 'g_ffn_post_2', 'w_ple_proj_2', 'w_ple_gate_2', 'g_ple_post_2']


def kernel(**inputs):
    import concourse.bacc as bacc
    from concourse.bass_utils import run_bass_kernel_spmd

    nc = bacc.Bacc("TRN2", target_bir_lowering=False, num_devices=1)
    arrays = {name: np.ascontiguousarray(inputs[name]) for name in INPUTS}
    arrays["const_first"], arrays["const_second"] = constants()
    io = {name: nc.dram_tensor(f"in_{name}", a.shape, F32, kind="ExternalInput").ap() for name, a in arrays.items()}
    io["out"] = nc.dram_tensor("out_0", (1, TOK, D), F32, kind="ExternalOutput").ap()
    sent = {name: [0, 0, 0] for name in SIGNALS}
    build(nc, io, SIGNALS, sent)
    assert sent == SIGNALS, "the table of signals doesn't fit the program"
    result = run_bass_kernel_spmd(nc, [{f"in_{name}": a for name, a in arrays.items()}], core_ids=[0])
    return result.results[0]["out_0"]
```

```python
from contextlib import ExitStack

import numpy as np

import concourse.bass as bass
from concourse import mybir

F32 = mybir.dt.float32
F32R = mybir.dt.float32r
ALU = mybir.AluOpType
ACT = mybir.ActivationFunctionType
AX = mybir.AxisListType

P = 128
TOK = 256
NT = TOK // P
D = 1024
KD = D // P
LAYERS = 2
COLS = 512

MLA_H, MLA_Q, MLA_KV, NOPE, ROPE, MLA_V = 8, 256, 128, 64, 32, 64
QK_D = NOPE + ROPE
MOBA_H, MOBA_D = 8, 64
MOBA_R = MOBA_D // 4
RET_H, RET_K, RET_V, RET_CHUNK = 4, 64, 128, 128
D_FF = 4 * D
IN1 = [MLA_Q, MLA_KV, ROPE] + [MOBA_H * MOBA_D] * 3 + [RET_H * RET_K] * 2 + [RET_H * RET_V] * 2 + [D] * 3
CQ, CKV, KR, MQ, MK, MV, RQ, RK, RV, RG, G_MLA, G_MOBA, G_RET = [int(sum(IN1[:i])) for i in range(len(IN1))]
IN1_COLS = sum(IN1)

GLA_H, GLA_K, GLA_V, GLA_R, GLA_CHUNK = 4, 128, 256, 16, 64
GLA_TAU = 16.0
AQ_H, AKV_H, A_D, GRID_W = 8, 2, 128, 64
FFN = 2816
PLE = 256
IN2 = [GLA_H * GLA_K] * 2 + [GLA_H * GLA_V] * 2 + [GLA_R] * 2 + [AQ_H * A_D, AKV_H * A_D, AKV_H * A_D, D, D]
GQ, GK, GV, GG, RA_F, RA_B, AQ, AK, AV, G_A, G_B = [int(sum(IN2[:i])) for i in range(len(IN2))]
IN2_COLS = sum(IN2)
RA = IN2_COLS - 2 * GLA_R


def at2(col):
    return col if col < RA_F else col - 2 * GLA_R


NORM_EPS, GN_EPS = 1e-6, 1e-5
NEG = -1e30

CONST_PARTS = [[
    ("ident", 128), ("causal", 384), ("decay", RET_H * 384),
    ("c_mla", NT * 16), ("s_mla", NT * 16), ("c_moba", NT * 8), ("s_moba", NT * 8),
    ("c_ret", NT * 32), ("s_ret", NT * 32),
], [
    ("ident", 128), ("c_ax", NT * 64), ("s_ax", NT * 64),
    ("cum_f", 128), ("cum_b", 128), ("rest_f", 128), ("rest_b", 128), ("in_f", 128), ("in_b", 128), ("halves", 2),
]]
CONST_AT = {n: (sum(w for _, w in part[:i]), w) for part in CONST_PARTS for i, (n, w) in enumerate(part)}
CONST_COLS = [sum(w for _, w in part) for part in CONST_PARTS]


def constants():
    f = np.float32
    j, i = np.arange(P)[:, None], np.arange(P)[None, :]
    out = {"ident": np.eye(P, dtype=f)}
    tri = np.where(i <= j, 0.0, NEG).astype(f)
    out["causal"] = np.concatenate([np.zeros((P, P), f), tri, tri], 1)
    lg = np.log(1.0 - 2.0 ** (-5.0 - np.arange(RET_H)))
    wide = np.arange(TOK)[None, :] - np.arange(P)[:, None]
    dec = [np.where(wide >= 0, np.exp(g * np.maximum(wide, 0)), 0.0) * RET_K ** -0.5 for g in lg]
    out["decay"] = np.concatenate([np.concatenate([d, d[:, :P]], 1) for d in dec], 1)

    def rope(dim, theta):
        inv = (1.0 / (f(theta) ** (np.arange(0, dim, 2, dtype=f) / f(dim)))).astype(f)
        ang = (np.arange(TOK, dtype=f)[:, None] * inv[None, :]).astype(f)
        return np.cos(ang), np.sin(ang)

    def by_tile(a):
        return a.reshape(NT, P, -1).transpose(1, 0, 2).reshape(P, -1)

    for n, dim, theta in (("mla", ROPE, 500000.0), ("moba", MOBA_R, 500000.0), ("ret", RET_K, 10000.0)):
        c, s = rope(dim, theta)
        out["c_" + n], out["s_" + n] = by_tile(c), by_tile(s)
    axis = A_D // 2
    row = np.repeat(np.arange(TOK // GRID_W, dtype=f), GRID_W)
    col = np.tile(np.arange(GRID_W, dtype=f), TOK // GRID_W)
    inv = (f(10000.0) ** (-np.arange(0, axis, 2, dtype=f) / f(axis))).astype(f)
    ang = np.stack([row[:, None] * inv, col[:, None] * inv], 1)
    out["c_ax"], out["s_ax"] = by_tile(np.cos(ang)), by_tile(np.sin(ang))
    same = (j // GLA_CHUNK) == (i // GLA_CHUNK)
    out["cum_f"], out["cum_b"] = same * (j <= i) / GLA_TAU, same * (j >= i) / GLA_TAU
    out["rest_f"], out["rest_b"] = same * (j > i) / GLA_TAU, same * (j < i) / GLA_TAU
    out["in_f"], out["in_b"] = same * (j <= i), same * (j >= i)
    out["halves"] = (j // GLA_CHUNK == np.arange(P // GLA_CHUNK)[None, :]) / GLA_TAU
    return [np.ascontiguousarray(np.concatenate([np.asarray(out[n], f) for n, _ in part], 1)) for part in CONST_PARTS]


RING = 4


class Chunk:
    def __init__(self, name, weight, act, k_tiles, col, n, wide=False, to=0):
        self.name, self.weight, self.act, self.k_tiles = name, weight, act, k_tiles
        self.col, self.n, self.wide, self.to = col, n, wide, to
        self.units = k_tiles if wide or k_tiles == 1 else k_tiles // 2


def chunks_first():
    c = [Chunk("p", "w_in", "xT", KD, 0, MQ, to=0)]
    c += [Chunk("p", "w_in", "xT", KD, x, COLS, to=x) for x in range(MQ, G_MLA, COLS)]
    c += [Chunk("q_up", "mla_w_q_up", "cT", 2, 0, COLS, to=0),
          Chunk("q_up", "mla_w_q_up", "cT", 2, COLS, MLA_H * QK_D - COLS, to=COLS)]
    c += [Chunk("kv_up", "mla_w_kv_up", "kvT", 1, x, COLS, to=x // 128) for x in (0, COLS)]

    def gate(g):
        return [Chunk("gate", "w_in", "xT", KD, x, COLS, to=x) for x in (g, g + COLS)]

    def branch(n):
        return [Chunk("branch_" + n, "w_branch_" + n, "oT", 4, x, COLS, to=x) for x in (0, COLS)]

    c += gate(G_MLA) + gate(G_RET) + branch("mla") + gate(G_MOBA) + branch("ret") + branch("moba")
    c += [Chunk("residual", "w_out", "xT", KD, x, COLS, to=x) for x in (0, COLS)]
    c += [Chunk("up", "w_mlp_up", "xT", KD, x, COLS, to=4 * (x // COLS)) for x in range(0, D_FF, COLS)]
    c += [Chunk("residual_wide", "w_mlp_down", "hT", D_FF // P, 0, D, wide=True)]
    return c


def chunks_second():
    def p(first, end, n=COLS, to=None):
        return [Chunk("p", "w_in_2", "xT", KD, x, n, to=at2(x) if to is None else to) for x in range(first, end, n)]

    c = p(GQ, GV) + p(RA_F, AQ, 2 * GLA_R, RA) + p(GV, RA_F) + p(AQ, G_A)
    c += [Chunk("gate", "w_in_2", "xT", KD, x, COLS, to=at2(x)) for x in range(G_A, IN2_COLS, COLS)]
    c += [Chunk("branch_gla", "w_o_gla_2", "xT", KD, x, COLS, to=x) for x in (0, COLS)]
    c += [Chunk("branch_attn", "w_o_attn_2", "xT", KD, x, COLS, to=x) for x in (0, COLS)]
    c += [Chunk("normed", "w_out_2", "xT", KD, x, COLS, to=x) for x in (0, COLS)]
    for x in range(0, FFN, COLS):
        n = min(COLS, FFN - x)
        c += [Chunk("glu_gate", "w_ffn_in_2", "xT", KD, x, n, to=x // P), Chunk("glu_up", "w_ffn_in_2", "xT", KD, FFN + x, n, to=x // P)]
    c += [Chunk("normed_wide", "w_ffn_out_2", "hT", FFN // P, 0, D, wide=True)]
    c += [Chunk("plain_wide", "w_ple_proj_2", "pT", PLE // P, 0, D, wide=True)]
    c += [Chunk("ple", "w_ple_gate_2", "xT", KD, x, COLS, to=x) for x in (0, COLS)]
    return c


SIGNALS = {
    'unit_used'         : [140, 0, 160],
    'hi_ready'          : [140, 0, 160],
    'lo_ready'          : [140, 0, 160],
    'rows_ready'        : [26, 0, 34],
    'prob_ready'        : [16, 0, 0],
    'half_ready'        : [36, 0, 36],
    'variance'          : [4, 1, 8],
    'root_ready'        : [4, 1, 8],
    'norm_open'         : [8, 4, 12],
    'squared'           : [8, 4, 20],
    'table_loaded'      : [1, 0, 3],
    'logarithm'         : [0, 0, 2],
    'shift_ready'       : [16, 0, 8],
    'silu_ready'        : [1, 0, 1],
    'gates_ready'       : [2, 0, 0],
    'rotated'           : [1, 0, 0],
    'dve_step'          : [44, 4, 86],
    'params_free'       : [1, 0, 1],
    'params_loaded'     : [4, 0, 4],
    'step_open'         : [17, 0, 0],
    'minus_abs'         : [0, 0, 2],
    'decays_ready'      : [0, 0, 2],
    'softplus'          : [0, 0, 2],
    'walpha_used'       : [0, 0, 1],
    'walpha_loaded'     : [0, 0, 1],
    'states_ready'      : [0, 0, 4],
    'gg_ready'          : [0, 0, 1],
    'heads_done'        : [0, 0, 1],
    'pe_rows_loaded'    : [0, 0, 1],
    'glu_ready'         : [0, 0, 6],
    'bank0_drained'     : [25, 0, 27],
    'bank0_filled'      : [25, 0, 27],
    'bank1_drained'     : [27, 0, 28],
    'bank1_filled'      : [27, 0, 28],
    'bank2_drained'     : [22, 0, 27],
    'bank2_filled'      : [22, 0, 27],
    'bank3_drained'     : [18, 0, 26],
    'bank3_filled'      : [18, 0, 26],
    'gain0_free'        : [1, 0, 2],
    'gain0_loaded'      : [1, 0, 2],
    'gain1_free'        : [1, 0, 2],
    'gain1_loaded'      : [1, 0, 2],
    'gain2_free'        : [0, 1, 1],
    'gain2_loaded'      : [0, 1, 1],
    'pair0_drained'     : [18, 0, 19],
    'pair1_drained'     : [17, 0, 19],
    'raw0_loaded'       : [35, 0, 40],
    'raw1_loaded'       : [35, 0, 40],
    'raw2_loaded'       : [35, 0, 40],
    'raw3_loaded'       : [35, 0, 40],
}


FIRST, BETWEEN, SECOND = 0, 1, 2
REPEATS = [LAYERS, 1, LAYERS]


class Plan:

    def __init__(self, chunks):
        self.chunks = chunks
        self.unit = []
        uses = [0, 0]
        weights = set()
        turn = 0
        for i, c in enumerate(chunks):
            c.first = len(self.unit)
            self.unit += [(i, n) for n in range(c.units)]
            c.last = len(self.unit) - 1
            c.fresh = c.weight not in weights
            weights.add(c.weight)
            c.pairs = [0, 1] if c.wide else [turn % 2]
            turn += 0 if c.wide else 1
            c.use = [uses[x] for x in c.pairs]
            for x in c.pairs:
                uses[x] += 1
        self.n = len(self.unit)
        assert self.n % RING == 0
        self.ends = {c.last: c for c in chunks}

    def ended(self, u, after, before):
        return self.ends.get(u) if after <= u < before else None


class Stream:

    def __init__(self, plan, unit, follow):
        self.plan, self.unit, self.follow, self.u, self.after = plan, unit, follow, 0, 0

    def run(self, count):
        for _ in range(count):
            self.unit(self.u)
            self.trail(self.u)
            self.u += 1

    def trail(self, u):
        for delay, step in self.follow:
            c = self.plan.ended(u - delay, self.after, self.u + 1 if u == self.u else self.u)
            if c is not None:
                step(c)

    def finish(self):
        for u in range(self.u, self.u + 1 + max(d for d, _ in self.follow)):
            self.trail(u)
        self.after = self.u


class Counts:

    def __init__(self, sems, totals, credit, sent):
        self.sems, self.totals, self.credit, self.sent = sems, totals, credit, sent
        self.segment, self.layer, self.seen, self.own = 0, 0, {}, {}

    def enter(self, segment, Ler):
        self.segment, self.layer, self.seen, self.own = segment, Ler, {}, {}

    def at(self, name, n):
        t = self.totals[name]
        before = sum(t[s] * REPEATS[s] for s in range(self.segment))
        return self.sems[name], self.layer * t[self.segment] + (before + n + self.credit.get(name, 0))

    def dma(self, name, n):
        sem, value = self.at(name, n)
        return sem, value * 16

    def next(self, name, n=1):
        self.seen[name] = self.seen.get(name, 0) + n
        return self.at(name, self.seen[name])

    def up(self, name, count=1):
        self.own[name] = self.own.get(name, 0) + count
        self.sent[name][self.segment] += count
        return self.sems[name], count


ONCE = ["x_loaded", "ident_loaded", "const_loaded", "ring_clear", "result_ready", "stored"]
CREDIT = {"pair0_drained": 1, "pair1_drained": 1, "lo_ready": 4, "unit_used": 4, "squared": 4,
          **{f"bank{b}_drained": 1 for b in range(4)}, **{f"gain{s}_free": 1 for s in range(3)}, "params_free": 1, "walpha_used": 1}
GAIN_SLOT = {FIRST: [0, 1], BETWEEN: [2], SECOND: [0, 1, 0, 1, 2]}
EVAC, TURN = 1, 3


def spread(ap, axis, count):
    shape = list(ap.shape)
    return ap.unsqueeze(axis).broadcast_to(shape[:axis] + [count] + shape[axis:])


QUARTERS = [(g, t) for g in range(2) for t in range(NT)]
IN_QUARTERS = ("w_in", "w_out", "w_mlp_up", "w_in_2", "w_o_gla_2", "w_o_attn_2", "w_out_2", "w_ffn_in_2", "w_ple_gate_2")


class Banks:

    def __init__(self):
        self.given, self.uses, self.turn = {}, [0] * 4, 0

    def get(self, key, among=(0, 1, 2, 3)):
        if key not in self.given:
            b = among[self.turn % len(among)]
            self.turn += 1
            self.given[key] = (b, self.uses[b])
            self.uses[b] += 1
        return self.given[key]


class Layout:
    pass


def build(nc, io, totals, sent):
    ctx = ExitStack()
    with ctx:
        def sb(name, shape, dt=F32):
            return ctx.enter_context(nc.sbuf_tensor(name, shape, dt))

        raw = sb("raw", [P, RING, 2, COLS])
        hi = sb("hi", [P, RING, 2, COLS], F32R)
        lo = sb("lo", [P, RING, 2, COLS], F32R)
        x = sb("x", [P, NT, D])
        y = sb("y", [P, NT, D])
        xT = [sb(f"xT{i}", [P, KD, TOK], F32R) for i in "hl"]
        gains = sb("gains", [P, 3, D])
        params = sb("params", [P, 1536])
        const = sb("const", [P, max(CONST_COLS)])
        small = sb("small", [P, 256])
        tmp = sb("tmp", [P, 1024])
        big = nc.sbuf_usable_end // 32 * 32 - 2 * 32 * TOK * 4
        hT = [nc.alloc_sbuf_tensor_at(f"hT{i}", [P, 32, TOK], F32R, offset=big + n * 32 * TOK * 4)
              for n, i in enumerate("hl")]
        proj = nc.alloc_sbuf_tensor_at("proj", [P, NT, IN2_COLS], F32, offset=big)
        spare = big + NT * IN2_COLS * 4
        arena = big - 30 * 1024
        assert nc.sbuf_base <= arena and spare + 10240 <= nc.sbuf_usable_end, (nc.sbuf_base, arena)

        def at(name, kib, shape, dt=F32, base=arena):
            return nc.alloc_sbuf_tensor_at(name, shape, dt, offset=base + int(kib * 1024))

        qT = at("qT", 0, [P, 8, TOK])
        kT = at("kT", 8, [P, 8, TOK])
        prob = at("prob", 16, [P, 2, 384])
        probT = at("probT", 19, [P, 2, 384])
        oT = [at("oTh", 22, [P, 4, TOK], F32R), at("oTl", 26, [P, 4, TOK], F32R)]
        km = at("km", 0, [P, NT, MLA_H, QK_D], base=spare)
        vm = at("vm", 6, [P, NT, MLA_H, MLA_V], base=spare)

        states = at("states", 16, [P, 2, 3, GLA_V])
        raT = at("raT", 16, [GLA_R, 2, TOK])
        qd = at("qd", 22, [P, NT, COLS])
        kd = at("kd", 26, [P, NT, COLS])
        seenT = at("seenT", 22, [P, 2, 2, NT, P])
        ks = at("ks", 0, [P, 2, NT, COLS], base=spare)
        silu = at("silu", 0, [P, NT, D], base=spare)
        wide = at("wide", 0, [P, 4 * D])
        soft = at("soft", 0, [P, 2, NT, COLS])
        attn = at("attn", 16, [P, 2, NT, TOK])
        attnT = at("attnT", 22, [P, 2, 4, P])
        pe_rows = at("pe_rows", 16, [P, NT, PLE])

        acc = ctx.enter_context(nc.psum_tensor("acc", [P, 4, COLS], F32))
        mix = ctx.enter_context(nc.psum_tensor("mix", [P, 4, COLS], F32))

        def cst(name, *shape):
            a, w = CONST_AT[name]
            v = const[:, a:a + w]
            if len(shape) == 2:
                v = v.rearrange("p (a b) -> p a b", a=shape[0])
            return v

        ident = cst("ident")
        sems = {name: ctx.enter_context(nc.semaphore(name)) for name in [*totals, *ONCE]}
        plans = {FIRST: Plan(chunks_first()), SECOND: Plan(chunks_second())}
        banks = {s: Banks() for s in (FIRST, BETWEEN, SECOND)}
        acts = {"xT": xT, "hT": hT, "oT": oT, "cT": oT, "kvT": [a[:, 2:3] for a in oT], "pT": oT}
        L = Layout()
        L.acc, L.acts, L.attn, L.attnT, L.banks, L.const, L.cst, L.gains = acc, acts, attn, attnT, banks, const, cst, gains
        L.hT, L.hi, L.ident, L.kT, L.kd, L.km, L.ks, L.lo = hT, hi, ident, kT, kd, km, ks, lo
        L.mix, L.oT, L.params, L.pe_rows, L.plans, L.prob, L.probT, L.proj = mix, oT, params, pe_rows, plans, prob, probT, proj
        L.qT, L.qd, L.raT, L.raw, L.seenT, L.sems, L.silu, L.small = qT, qd, raT, raw, seenT, sems, silu, small
        L.soft, L.states, L.tmp, L.vm, L.wide, L.x, L.xT, L.y = soft, states, tmp, vm, wide, x, xT, y
        block = ctx.enter_context(nc.Block())

        def counts():
            return Counts(sems, totals, CREDIT, sent)

        @block.tensor
        def _(pe):
            tensor_program(nc, pe, counts(), L)

        @block.sync
        def _(sp):
            sync_program(nc, sp, counts(), L, io)

        @block.gpsimd
        def _(pool):
            gpsimd_program(nc, pool, counts(), L)

        @block.scalar
        def _(act):
            scalar_program(nc, act, counts(), L, io)

        @block.vector
        def _(dve):
            vector_program(nc, dve, counts(), L)


KV_BANKS = (((0, 0), (0, 2)), ((0, 1), (1, 3)), ((1, 2),), ((1, 1),))
LAST_INTER = ((0, 2), (1, 2))


def tensor_program(nc, pe, n, L):
    seg = FIRST

    def fill(key, products, among=(0, 1, 2, 3)):
        b, use = L.banks[seg].get(key, among)
        pe.wait_ge(*n.at(f"bank{b}_drained", use))
        for last in products(b):
            pass
        last.then_inc(*n.up(f"bank{b}_filled"))

    def emptied(key):
        b, use = L.banks[seg].get(key)
        pe.wait_ge(*n.at(f"bank{b}_drained", use + 1))

    def turn(key, rows, tiles, width=P, among=(0, 1, 2, 3)):
        def products(b):
            for i, k in enumerate(tiles):
                for t in range(NT):
                    yield nc.tensor.transpose(L.mix[0:width, b, i * TOK + t * P:i * TOK + (t + 1) * P], rows(t, k), L.ident)
        fill(key, products, among)

    def turn_all(weight, rows, k_tiles):
        if weight in IN_QUARTERS:
            for g, t in QUARTERS:
                pe.wait_ge(*n.next("rows_ready"))
                fill((weight, g, t), lambda b: [nc.tensor.transpose(L.mix[:, b, i * P:(i + 1) * P], rows(t, 4 * g + i), L.ident) for i in range(4)])
            return
        pe.wait_ge(*n.next("rows_ready"))
        for j in range(0, k_tiles, 2):
            turn((weight, j // 2), rows, range(j, min(j + 2, k_tiles)))

    def unit(u):
        plan = L.plans[seg]
        ci, j = plan.unit[u]
        c = plan.chunks[ci]
        slot = u % RING
        if j == 0:
            for pair, use in zip(c.pairs, c.use):
                pe.wait_ge(*n.at(f"pair{pair}_drained", use))
        if c.fresh and (not c.wide or j % 2 == 0):
            for key in [(c.weight, j // 2, t) for t in range(NT)] if c.weight in IN_QUARTERS else [(c.weight, j // 2 if c.wide else j)]:
                emptied(key)
        pe.wait_ge(*n.at("hi_ready", u + 1))
        pe.wait_ge(*n.at("lo_ready", u + 1))
        ah, al = L.acts[c.act]
        for part in range(2 if c.wide or c.k_tiles > 1 else 1):
            k = j if c.wide else 2 * j + part
            for t in range(NT):
                out = L.acc[:, (2 * part if c.wide else 2 * c.pairs[0]) + t, 0:c.n if not c.wide else COLS]
                for a, w in ((ah, L.hi), (ah, L.lo), (al, L.hi)):
                    last = nc.tensor.matmul(out, a[:, k, t * P:(t + 1) * P], w[:, slot, part, 0:out.shape[1]],
                                            start=(k == 0 and a is ah and w is L.hi),
                                            stop=(k == c.k_tiles - 1 and a is al))
        last.then_inc(*n.up("unit_used"))

    def scores(tag, h, q, k):
        def products(b):
            for a, w, c in ((P, TOK, 0), (0, P, TOK)):
                yield nc.tensor.matmul(L.mix[:, b, c:c + w], q[:, a:a + P], k[:, 0:w], start=True, stop=True)
        fill((tag, "s", h), products, (0, 1, 2))

    def prob_turn(tag, h):
        pe.wait_ge(*n.next("prob_ready"))
        def products(b):
            for i in range(3):
                yield nc.tensor.transpose(L.mix[:, b, i * P:(i + 1) * P], L.prob[:, h % 2, i * P:(i + 1) * P], L.ident)
        fill((tag, "t", h), products, (0, 1, 2))

    def context(tag, h, v, dv, blocks, per):
        g, i = h // per, h % per
        b, use = L.banks[seg].get((tag, "o", g), (3,))
        if i == 0:
            pe.wait_ge(*n.at(f"bank{b}_drained", use))
        for t in range(NT):
            for kt in range(t + 1):
                c = blocks[t, kt]
                last = nc.tensor.matmul(L.mix[:, b, (t * per + i) * dv:(t * per + i + 1) * dv],
                                        L.probT[:, h % 2, c:c + P], v(kt, h), start=(kt == 0), stop=(kt == t))
        if i == per - 1:
            last.then_inc(*n.up(f"bank{b}_filled"))

    def softmax_heads(tag, heads, q, k, v, s, units):
        blocks = {(1, 0): 0, (1, 1): P, (0, 0): TOK}
        for h in range(heads + 2):
            if h < heads:
                scores(tag, h, q(h), k(h))
            if h >= 2:
                emptied((tag, "t", h - 2))
                context(tag, h - 2, v, MLA_V, blocks, 4)
            s.run(units[h] if h < len(units) else 0)
            if 1 <= h <= heads:
                prob_turn(tag, h - 1)

    def hidden_turn(c):
        if c.name == "up" or c.name == "glu_up":
            weight = "w_mlp_down" if c.name == "up" else "w_ffn_out_2"
            pe.wait_ge(*n.next("rows_ready"))
            slot = (c.to // 4) % 2
            for j in range(0, c.n // P, 2):
                turn((weight, (c.to + j) // 2), lambda t, k: L.y[:, t, slot * COLS + k * P:slot * COLS + (k + 1) * P], range(j, j + 2))

    def first_layer():
        s = Stream(L.plans[FIRST], unit, [(TURN, hidden_turn)])
        x_rows = lambda t, k: L.y[:, t, k * P:(k + 1) * P]
        turn_all("w_in", x_rows, KD)
        s.run(10)
        pe.wait_ge(*n.next("rows_ready"))
        latent = lambda t, k: L.proj[:, t, k * P:(k + 1) * P]
        turn(("mla_w_q_up", 0), latent, (0, 1))
        turn(("mla_w_kv_up", 0), latent, (2,))
        s.run(24 - 6 + 4 + 2)
        pe.wait_ge(*n.next("rows_ready"))
        for j in range(4):
            turn(("mla", "q", j), lambda t, h: L.y[:, t, h * QK_D:(h + 1) * QK_D], (2 * j, 2 * j + 1), QK_D)
        for j in range(4):
            turn(("mla", "k", j), lambda t, h: L.km[:, t, h, :], (2 * j, 2 * j + 1), QK_D)
        for j in range(4):
            emptied(("mla", "q", j)); emptied(("mla", "k", j))
        softmax_heads("mla", MLA_H, lambda h: L.qT[0:QK_D, h, :], lambda h: L.kT[0:QK_D, h, :],
                      lambda t, h: L.vm[:, t, h, :], s, [2, 2, 1, 2, 1, 2, 1, 2, 1, 0])
        pe.wait_ge(*n.next("rows_ready"))
        for w, col in (("q", RQ), ("k", RK)):
            turn(("ret", w, 0), lambda t, k: L.proj[:, t, col + k * P:col + (k + 1) * P], (0, 1))
        turn_all("w_branch_mla", x_rows, 4)
        emptied(("ret", "q", 0)); emptied(("ret", "k", 0))
        for h in range(RET_H + 1):
            if h < RET_H:
                lo_p = RET_K * (h % 2)
                q, k = (a[lo_p:lo_p + RET_K, h // 2, :] for a in (L.qT, L.kT))
                def products(b, q=q, k=k):
                    for kt, w, c in ((0, TOK, 0), (1, P, TOK)):
                        yield nc.tensor.matmul(L.mix[:, b, c:c + w], k[:, kt * P:(kt + 1) * P], q[:, kt * P:TOK], start=True, stop=True)
                fill(("ret", "s", h), products, (0, 1, 2))
            s.run(1 if h else 0)
            if h:
                emptied(("ret", "s", h - 1))
                context("ret", h - 1, lambda t, hh: L.proj[:, t, RV + hh * RET_V:RV + (hh + 1) * RET_V], RET_V,
                        {(0, 0): 0, (1, 0): P, (1, 1): TOK}, 2)
        for w, col in (("q", MQ), ("k", MK)):
            for j in range(2):
                turn(("moba", w, j), lambda t, k: L.proj[:, t, col + k * P:col + (k + 1) * P], (2 * j, 2 * j + 1))
        for w in "qk":
            for j in range(2):
                emptied(("moba", w, j))
        half = lambda a, h: a[MOBA_D * (h % 2):MOBA_D * (h % 2 + 1), h // 2, :]
        heads = lambda units: softmax_heads("moba", MOBA_H, lambda h: half(L.qT, h), lambda h: half(L.kT, h),
                      lambda t, h: L.proj[:, t, MV + h * MOBA_D:MV + (h + 1) * MOBA_D], s, units)
        heads([1, 1, 1, 1, 1, 1, 1, 1, 0, 0])
        turn_all("w_branch_ret", lambda t, k: L.y[:, t, COLS + k * P:COLS + (k + 1) * P], 4)
        s.run(4)
        turn_all("w_branch_moba", x_rows, 4)
        s.run(4)
        turn_all("w_out", lambda t, k: L.proj[:, t, G_MLA + k * P:G_MLA + (k + 1) * P], KD)
        s.run(8)
        turn_all("w_mlp_up", x_rows, KD)
        s.run(32)
        s.finish()
        s.run(32)
        assert s.u == L.plans[FIRST].n

    def second_layer():
        s = Stream(L.plans[SECOND], unit, [(TURN, hidden_turn)])
        y_rows = lambda t, k: L.y[:, t, k * P:(k + 1) * P]
        f32 = dict(start=True, stop=True)
        turn_all("w_in_2", y_rows, KD)
        s.run(14)
        pe.wait_ge(*n.next("rows_ready"))
        def ra_blocks(b):
            for d in range(2):
                for t in range(NT):
                    yield nc.tensor.transpose(L.mix[0:GLA_R, b, d * TOK + t * P:d * TOK + (t + 1) * P],
                                              L.proj[:, t, RA + d * GLA_R:RA + (d + 1) * GLA_R], L.ident)
        fill(("gla", "ra"), ra_blocks)
        s.run(2)
        emptied(("gla", "ra"))
        pe.wait_ge(*n.dma("walpha_loaded", 1))
        for d in range(2):
            for t in range(NT):
                fill(("gla", "z", d, t), lambda b: [nc.tensor.matmul(L.mix[:, b, :], L.raT[:, d, t * P:(t + 1) * P],
                                                                    L.tmp[0:GLA_R, d * COLS:(d + 1) * COLS], **f32)])
        s.run(4)
        for d in range(2):
            pe.wait_ge(*n.next("decays_ready"))
            for t in range(NT):
                for what in ("cum", "rest"):
                    fill(("gla", what, d, t), lambda b: [nc.tensor.matmul(L.mix[:, b, :], L.cst(f"{what}_{'fb'[d]}"),
                                                                         L.y[:, t, d * COLS:(d + 1) * COLS], **f32)])
            def chunk_sums(b):
                for h in range(GLA_H):
                    for t in range(NT):
                        yield nc.tensor.matmul(L.mix[:, b, 4 * h + 2 * t:4 * h + 2 * t + 2], L.y[:, t, d * COLS + h * P:d * COLS + (h + 1) * P], L.cst("halves"), **f32)
            fill(("gla", "last", d), chunk_sums)
            s.run(3)
            pe.wait_ge(*n.next("rows_ready"))
            for w, rows in (("q", L.qd), ("k", L.kd)):
                for j in range(2):
                    turn(("gla", w, d, j), lambda t, h: rows[:, t, h * P:(h + 1) * P], (2 * j, 2 * j + 1))
            s.run(2)
        for d in range(2):
            for j in range(2):
                emptied(("gla", "q", d, j)); emptied(("gla", "k", d, j))

        def gla_head(h):
            gv = lambda r, t: L.proj[r, t, at2(GV) + h * GLA_V:at2(GV) + (h + 1) * GLA_V]
            def seen(b):
                for d in range(2):
                    for t in range(NT):
                        yield nc.tensor.matmul(L.mix[:, b, d * TOK + t * P:d * TOK + (t + 1) * P],
                                               L.kT[:, 4 * d + h, t * P:(t + 1) * P], L.qT[:, 4 * d + h, t * P:(t + 1) * P], **f32)
            fill(("gla", "s", h), seen)
            for i, pairs in enumerate(KV_BANKS):
                def kv(b):
                    for m, (d, c) in enumerate(pairs):
                        r = slice(GLA_CHUNK * (c % 2), GLA_CHUNK * (c % 2 + 1))
                        yield nc.tensor.matmul(L.mix[:, b, m * GLA_V:(m + 1) * GLA_V], L.ks[r, d, c // 2, h * P:(h + 1) * P], gv(r, c // 2), **f32)
                fill(("gla", "kv", h, i), kv)
            s.run(2)
            emptied(("gla", "s", h))
            pe.wait_ge(*n.next("states_ready"))
            def out(b):
                for t in range(NT):
                    o = L.mix[:, b, t * GLA_V:(t + 1) * GLA_V]
                    for d in range(2):
                        yield nc.tensor.matmul(o, L.seenT[:, h % 2, d, t, :], gv(slice(0, P), t), start=(d == 0), stop=False)
                    inter = [(c, d, i) for c in (2 * t, 2 * t + 1) for d, i in ((0, c - 1), (1, 2 - c)) if i >= 0]
                    for m, (c, d, i) in enumerate(inter):
                        r = GLA_CHUNK * (c % 2)
                        yield nc.tensor.matmul(o[r:r + GLA_CHUNK], L.qT[:, 4 * d + h, c * GLA_CHUNK:(c + 1) * GLA_CHUNK],
                                               L.states[:, d, i, :], start=False, stop=(m in LAST_INTER[t]))
            fill(("gla", "o", h), out)
            s.run(1)

        for h in range(GLA_H):
            gla_head(h)
        s.run(14)
        turn_all("w_o_gla_2", y_rows, KD)
        pe.wait_ge(*n.next("rows_ready"))
        for j in range(4):
            turn(("gqa", "q", j), lambda t, k: L.proj[:, t, at2(AQ) + k * P:at2(AQ) + (k + 1) * P], (2 * j, 2 * j + 1))
        turn(("gqa", "k", 0), lambda t, k: L.proj[:, t, at2(AK) + k * P:at2(AK) + (k + 1) * P], (0, 1))
        for j in range(4):
            emptied(("gqa", "q", j))
        emptied(("gqa", "k", 0))
        for h in range(AQ_H + 2):
            if h < AQ_H:
                kv = h // (AQ_H // AKV_H)
                fill(("gqa", "s", h), lambda b: [nc.tensor.matmul(L.mix[:, b, t * TOK:(t + 1) * TOK], L.qT[:, h, t * P:(t + 1) * P],
                                                                 L.kT[:, kv, :], **f32) for t in range(NT)], (0, 1, 2))
            if h >= 2:
                g, i, kv = (h - 2) // 2, h % 2, (h - 2) // (AQ_H // AKV_H)
                b, use = L.banks[seg].get(("gqa", "o", g), (3,))
                emptied(("gqa", "t", h - 2))
                if i == 0:
                    pe.wait_ge(*n.at(f"bank{b}_drained", use))
                for t in range(NT):
                    for kt in range(NT):
                        last = nc.tensor.matmul(L.mix[:, b, (2 * t + i) * P:(2 * t + i + 1) * P], L.attnT[:, h % 2, 2 * t + kt, :],
                                                L.proj[:, kt, at2(AV) + kv * P:at2(AV) + (kv + 1) * P], start=(kt == 0), stop=(kt == NT - 1))
                if i == 1:
                    last.then_inc(*n.up(f"bank{b}_filled"))
            s.run(1 if 1 <= h <= 8 else 0)
            if 1 <= h <= AQ_H:
                emptied(("gqa", "s", h - 1))
                fill(("gqa", "t", h - 1), lambda b: [nc.tensor.transpose(L.mix[:, b, (2 * t + kt) * P:(2 * t + kt + 1) * P],
                     L.attn[:, (h - 1) % 2, t, kt * P:(kt + 1) * P], L.ident) for t in range(NT) for kt in range(NT)], (0, 1, 2))
        turn_all("w_o_attn_2", y_rows, KD)
        s.run(8)
        turn_all("w_out_2", lambda t, k: L.proj[:, t, at2(G_A) + k * P:at2(G_A) + (k + 1) * P], KD)
        s.run(8)
        turn_all("w_ffn_in_2", y_rows, KD)
        s.run(48)
        s.finish()
        s.run(20)
        pe.wait_ge(*n.dma("pe_rows_loaded", 1))
        turn(("w_ple_proj_2", 0), lambda t, k: L.pe_rows[:, t, k * P:(k + 1) * P], (0, 1))
        s.run(4)
        turn_all("w_ple_gate_2", lambda t, k: L.x[:, t, k * P:(k + 1) * P], KD)
        s.run(8)
        assert s.u == L.plans[SECOND].n

    pe.sem_inc(L.sems["unit_used"], CREDIT["unit_used"])
    pe.wait_ge(L.sems["ident_loaded"], 16)
    with pe.Fori(0, LAYERS) as layer:
        n.enter(FIRST, layer)
        first_layer()
    seg = SECOND
    pe.wait_ge(L.sems["const_loaded"], 32)
    with pe.Fori(0, LAYERS) as layer:
        n.enter(SECOND, layer)
        second_layer()


def sync_program(nc, sp, n, L, io):
    seg = FIRST

    def unit(u):
        plan = L.plans[seg]
        ci, j = plan.unit[u]
        c = plan.chunks[ci]
        slot = u % RING
        sp.wait_ge(*n.at("lo_ready", u - RING + 1))
        w = io[c.weight][n.layer]
        if c.wide:
            src, dst = w[j * P:(j + 1) * P, :], L.raw[:, slot].rearrange("p a b -> p (a b)")
        elif c.k_tiles == 1:
            src, dst = w[:, c.col:c.col + c.n], L.raw[:, slot, 0, 0:c.n]
        else:
            src = w[2 * j * P:(2 * j + 2) * P, c.col:c.col + c.n].rearrange("(k p) n -> p k n", p=P)
            dst = L.raw[:, slot, :, 0:c.n]
        sem, _ = n.up(f"raw{slot}_loaded")
        sp.dma_start(dst, src).then_inc(sem, 16)

    def gain(slot, row):
        sp.wait_ge(*n.at(f"gain{slot}_free", n.own.get(f"gain{slot}_loaded", 0)))
        sem, _ = n.up(f"gain{slot}_loaded")
        sp.dma_start(L.gains[:, slot], row.partition_broadcast(P)).then_inc(sem, 16)

    def narrow(parts):
        sp.wait_ge(*n.at("params_free", 0))
        col = 0
        for row in parts:
            sem, _ = n.up("params_loaded")
            sp.dma_start(L.params[:, col:col + row.shape[-1]], row.partition_broadcast(P)).then_inc(sem, 16)
            col += row.shape[-1]

    sp.dma_start(L.x[:, :, :], io["x"][0].rearrange("(t p) d -> p t d", p=P)).then_inc(L.sems["x_loaded"], 16)
    sp.dma_start(L.ident, io["const_first"][:, 0:P]).then_inc(L.sems["ident_loaded"], 16)
    sp.wait_ge(L.sems["ring_clear"], 1)
    with sp.Fori(0, LAYERS) as layer:
        n.enter(FIRST, layer)
        gain(0, io["attn_norm"][layer])
        s = Stream(L.plans[FIRST], unit, [(0, lambda c: None)])
        s.run(4)
        narrow([io[w][layer] for w in ("mla_q_norm", "mla_kv_norm", "ret_gn_w", "ret_gn_b")])
        gain(1, io["mlp_norm"][layer])
        s.run(s.plan.n - 4)
    n.enter(BETWEEN, 0)
    gain(2, io["final_norm"])
    seg = SECOND
    with sp.Fori(0, LAYERS) as layer:
        n.enter(SECOND, layer)
        gain(0, io["g_mix_pre_2"][layer])
        s = Stream(L.plans[SECOND], unit, [(0, lambda c: None)])
        s.run(4)
        narrow([io["g_gla_out_2"][layer], io["g_q_norm_2"][layer], io["g_k_norm_2"][layer],
                io["b_alpha_2"][layer].rearrange("a b -> (a b)")])
        sp.wait_ge(*n.at("walpha_used", 0))
        sp.dma_start(L.tmp[0:GLA_R, :].rearrange("r (d c) -> r d c", d=2), io["w_alpha_up_2"][layer].rearrange("d r c -> r d c"))\
            .then_inc(n.up("walpha_loaded")[0], 16)
        gain(1, io["g_mix_post_2"][layer])
        s.run(20)
        gain(0, io["g_ffn_pre_2"][layer])
        gain(2, io["g_ple_post_2"][layer])
        s.run(80)
        gain(1, io["g_ffn_post_2"][layer])
        sp.wait_ge(*n.at("heads_done", 1))
        sp.dma_start(L.pe_rows[:, :, :], io["p_2"][layer, 0].rearrange("(t p) d -> p t d", p=P)).then_inc(n.up("pe_rows_loaded")[0], 16)
        s.run(s.plan.n - 104)
    sp.wait_ge(L.sems["result_ready"], 1)
    sp.dma_start(io["out"][0].rearrange("(t p) d -> p t d", p=P), L.x[:, :, :]).then_inc(L.sems["stored"], 16)
    sp.wait_ge(L.sems["stored"], 16)


def gpsimd_program(nc, pool, n, L):
    pool.sem_inc(L.sems["lo_ready"], CREDIT["lo_ready"])
    for seg in (FIRST, SECOND):
        rounds = L.plans[seg].n // RING * REPEATS[seg]
        n.enter(seg, 0)
        for _ in range(L.plans[seg].n):
            n.up("lo_ready")
        start = 0 if seg == FIRST else L.plans[FIRST].n // RING * LAYERS
        with pool.Fori(start, start + rounds) as r:
            for slot in range(RING):
                u = r * RING + slot
                pool.wait_ge(L.sems[f"raw{slot}_loaded"], r * 16 + 16)
                pool.wait_ge(L.sems["hi_ready"], u + 1)
                nc.gpsimd.tensor_tensor(L.lo[:, slot], L.raw[:, slot], L.hi[:, slot].bitcast(F32),
                                        ALU.subtract).then_inc(L.sems["lo_ready"], 1)


VAR, ROOT, NEWTON, MAXIMUM, SHIFT, SUMS, INVERSE, STATS, MOMENTS, PARTS, UNREAD = 0, 32, 64, 96, 100, 104, 120, 136, 184, 200, 204
LASTS = 136
HALVES_AHEAD = 3


def scalar_program(nc, act, n, L, io):
    seg = FIRST

    def high(u):
        slot = u % RING
        act.wait_ge(*n.dma(f"raw{slot}_loaded", u // RING + 1))
        act.wait_ge(*n.at("unit_used", u - RING + 1))
        nc.scalar.activation(L.hi[:, slot], L.raw[:, slot], ACT.Copy).then_inc(*n.up("hi_ready"))

    def unit(u):
        if u + HALVES_AHEAD < L.plans[seg].n:
            high(u + HALVES_AHEAD)

    def filled(key):
        b, use = L.banks[seg].get(key)
        act.wait_ge(*n.at(f"bank{b}_filled", use + 1))
        return b

    def empty(key, dst, width, rows=P):
        b = filled(key)
        nc.scalar.activation(dst, L.mix[0:rows, b, 0:width], ACT.Copy).then_inc(*n.up(f"bank{b}_drained"))

    def halves(weight, first, k_tiles, dst, at=0):
        if weight in IN_QUARTERS:
            for g, t in QUARTERS:
                b = filled((weight, g, t))
                nc.scalar.activation(dst[:, 4 * g:4 * g + 4, t * P:(t + 1) * P], L.mix[:, b, :].rearrange("p (k i) -> p k i", k=4), ACT.Copy)\
                    .then_inc(*n.up("half_ready"))
            return
        for j in range(0, k_tiles, 2):
            w = min(2, k_tiles - j)
            b = filled((weight, (first + j) // 2))
            nc.scalar.activation(dst[:, at + first + j:at + first + j + w, :], L.mix[:, b, 0:w * TOK], ACT.Copy).then_inc(*n.up("half_ready"))

    def root(width):
        act.wait_ge(*n.next("variance"))
        nc.scalar.activation(L.small[:, ROOT:ROOT + width], L.small[:, VAR:VAR + width], ACT.Sqrt).then_inc(*n.up("root_ready"))

    def load_root():
        nc.scalar.activation(L.small[:, UNREAD:UNREAD + 1], L.ident[:, 0:1], ACT.Sqrt).then_inc(*n.up("table_loaded"))
        act.wait_ge(*n.next("table_loaded"))

    def square(src, scratch, g, t):
        return nc.scalar.activation(scratch[:, t, g * COLS:(g + 1) * COLS], src, ACT.Square, scale=D ** -0.5,
                                    accum_out=L.small[:, PARTS + 2 * g + t:PARTS + 2 * g + t + 1])

    def squares(rows, scratch, halves=(0, 1)):
        for g in halves:
            for t in range(NT):
                act.wait_ge(*n.next("norm_open"))
                square(rows[:, t, g * COLS:(g + 1) * COLS], scratch, g, t).then_inc(*n.up("squared"))

    def softmax_exp(tag, h, scale):
        act.wait_ge(*n.next("shift_ready"))
        g, i, s = h // 4, h % 4, h % 2
        for t, c, w in ((1, 0, TOK), (0, TOK, P)):
            p = L.prob[:, s, c:c + w]
            last = nc.scalar.activation(p, p, ACT.Exp, bias=L.small[:, SHIFT + 2 * s + 1 - t:SHIFT + 2 * s + 2 - t], scale=scale,
                                 accum_out=L.small[:, SUMS + 8 * g + 4 * t + i:SUMS + 8 * g + 4 * t + i + 1])
        last.then_inc(*n.up("prob_ready"))

    def softmax_heads(tag, heads, scale, s, units, beside=None):
        for h in range(heads + 2):
            if h < heads:
                softmax_exp(tag, h, scale)
            if beside:
                beside(h)
            s.run(units[h] if h < len(units) else 0)
            if 1 <= h <= heads:
                empty((tag, "t", h - 1), L.probT[:, (h - 1) % 2, :], 384)

    def gate(c):
        if c.name == "gate":
            act.wait_ge(*n.at("unit_used", c.last + 1))
            p = c.pairs[0]
            nc.scalar.activation(L.proj[:, :, c.to:c.to + COLS], L.acc[:, 2 * p:2 * p + 2, :], ACT.Copy if seg == FIRST else ACT.Sigmoid)\
                .then_inc(*n.up(f"pair{p}_drained"))
        elif c.name == "glu_gate":
            act.wait_ge(*n.at("unit_used", c.last + 1))
            p, slot = c.pairs[0], c.to // 4 % 2
            nc.scalar.activation(L.y[:, :, slot * COLS:slot * COLS + c.n], L.acc[:, 2 * p:2 * p + 2, 0:c.n], ACT.Sigmoid)\
                .then_inc(*n.up("glu_ready"))
        elif c.name == "ple":
            act.wait_ge(*n.at("unit_used", c.last + 1))
            p = c.pairs[0]
            nc.scalar.activation(L.proj[:, :, c.to:c.to + COLS], L.acc[:, 2 * p:2 * p + 2, :], ACT.Sigmoid)\
                .then_inc(*n.up(f"pair{p}_drained"))
            if c.to:
                load_root()
            squares(L.y, L.proj, (c.to // COLS,))
        elif c.name == "residual":
            if c.to == 0:
                load_root()
            squares(L.x, L.y, (c.to // COLS,))
        elif c.name == "residual_wide":
            squares(L.x, L.y)
        elif c.name in ("normed", "normed_wide"):
            for half in range(2) if c.wide else (c.to // COLS,):
                if c.to == half == 0 and not c.wide:
                    load_root()
                act.wait_ge(*n.at("unit_used", c.last + 1))
                for t in range(NT):
                    square(L.acc[:, 2 * half + t, :], L.proj, half, t).then_inc(*n.up("squared"))

    def sigmoids(*cols):
        for c in L.plans[seg].chunks:
            if c.name == "gate" and any(g <= c.to < g + D for g in cols):
                act.wait_ge(*n.at(f"pair{c.pairs[0]}_drained", c.use[0] + 1))
        for g in cols:
            last = nc.scalar.activation(L.proj[:, :, g:g + D], L.proj[:, :, g:g + D], ACT.Sigmoid)
        last.then_inc(*n.up("gates_ready"))

    def hidden(c):
        if c.name == "up" or c.name == "glu_up":
            halves("w_mlp_down" if c.name == "up" else "w_ffn_out_2", c.to, c.n // P, L.hT[0])

    def first_layer():
        s = Stream(L.plans[FIRST], unit, [(EVAC, gate), (TURN, hidden)])
        root(2)
        for u in range(HALVES_AHEAD - 1):
            high(u)
        halves("w_in", 0, KD, L.xT[0])
        high(HALVES_AHEAD - 1)
        s.run(10)
        root(4)
        halves("mla_w_q_up", 0, 2, L.oT[0])
        halves("mla_w_kv_up", 0, 1, L.oT[0], 2)
        s.run(24)
        for j in range(4):
            empty(("mla", "q", j), L.qT[0:QK_D, 2 * j:2 * j + 2, :], 2 * TOK, QK_D)
        softmax_heads("mla", MLA_H, QK_D ** -0.5, s, [2, 2, 1, 2, 1, 2, 1, 2, 1, 0])
        empty(("ret", "q", 0), L.qT[:, 0:2, :], 2 * TOK)
        halves("w_branch_mla", 0, 4, L.oT[0])
        s.run(1)
        act.wait_ge(*n.next("rotated"))
        nc.scalar.activation(L.tmp[:, :].rearrange("p (t c) -> p t c", t=NT), L.proj[:, :, RG:RG + COLS], ACT.Sigmoid)\
            .then_inc(*n.up("silu_ready"))
        sigmoids(G_MLA, G_RET)
        s.run(3)
        for j in range(2):
            empty(("moba", "q", j), L.qT[:, 2 * j:2 * j + 2, :], 2 * TOK)
        softmax_heads("moba", MOBA_H, MOBA_D ** -0.5, s, [1, 1, 1, 1, 1, 1, 1, 1, 0, 0],
                      lambda h: root(8) if h == 2 else None)
        halves("w_branch_ret", 0, 4, L.oT[0])
        s.run(1)
        sigmoids(G_MOBA)
        s.run(3)
        halves("w_branch_moba", 0, 4, L.oT[0])
        s.run(4)
        halves("w_out", 0, KD, L.xT[0])
        s.run(8)
        s.finish()
        root(2)
        halves("w_mlp_up", 0, KD, L.xT[0])
        s.run(32)
        s.finish()
        s.run(32)
        s.finish()

    def second_layer():
        s = Stream(L.plans[SECOND], unit, [(EVAC, gate), (TURN, hidden)])
        root(2)
        for u in range(HALVES_AHEAD - 1):
            high(u)
        halves("w_in_2", 0, KD, L.xT[0])
        high(HALVES_AHEAD - 1)
        s.run(14)
        empty(("gla", "ra"), L.raT[:, :, :], 2 * TOK, GLA_R)
        s.run(2)
        for d in range(2):
            act.wait_ge(*n.next("minus_abs"))
            nc.scalar.activation(L.soft[:, d], L.soft[:, d], ACT.Exp).then_inc(*n.up("logarithm"))
            s.run(1)
        for d in range(2):
            act.wait_ge(*n.next("logarithm"))
            nc.scalar.activation(L.soft[:, d], L.soft[:, d], ACT.Ln, bias=1.0).then_inc(*n.up("softplus"))
            s.run(1)
        for d in range(2):
            for t in range(NT):
                b = filled(("gla", "cum", d, t))
                nc.scalar.activation(L.qd[:, t, :], L.mix[:, b, :], ACT.Exp)
                nc.scalar.activation(L.kd[:, t, :], L.mix[:, b, :], ACT.Exp, scale=-1.0).then_inc(*n.up(f"bank{b}_drained"))
                b = filled(("gla", "rest", d, t))
                nc.scalar.activation(L.ks[:, d, t, :], L.mix[:, b, :], ACT.Exp).then_inc(*n.up(f"bank{b}_drained"))
            b = filled(("gla", "last", d))
            nc.scalar.activation(L.small[:, LASTS + 16 * d:LASTS + 16 * d + 16], L.mix[:, b, 0:16], ACT.Exp).then_inc(*n.up(f"bank{b}_drained"))
            s.run(3)
            for j in range(2):
                empty(("gla", "q", d, j), L.qT[:, 4 * d + 2 * j:4 * d + 2 * j + 2, :], 2 * TOK)
            s.run(2)
        for h in range(GLA_H):
            s.run(2)
            if h == 1:
                root(8)
            empty(("gla", "o", h), L.y[:, :, h * GLA_V:(h + 1) * GLA_V], 2 * GLA_V)
            s.run(1)
        act.wait_ge(*n.next("gg_ready"))
        nc.scalar.activation(L.silu[:, :, :], L.proj[:, :, at2(GG):at2(GG) + D], ACT.Sigmoid).then_inc(*n.up("silu_ready"))
        root(8)
        s.run(8)
        root(12)
        s.run(6)
        halves("w_o_gla_2", 0, KD, L.xT[0])
        s.finish()
        for j in range(4):
            empty(("gqa", "q", j), L.qT[:, 2 * j:2 * j + 2, :], 2 * TOK)
        for h in range(AQ_H + 2):
            if h < AQ_H:
                act.wait_ge(*n.next("shift_ready"))
                b, use = L.banks[seg].get(("gqa", "s", h))
                for t in range(NT):
                    last = nc.scalar.activation(L.attn[:, h % 2, t, :], L.mix[:, b, t * TOK:(t + 1) * TOK], ACT.Exp,
                                                bias=L.small[:, SHIFT + 2 * (h % 2) + t:SHIFT + 2 * (h % 2) + t + 1], scale=A_D ** -0.5,
                                                accum_out=L.small[:, SUMS + 4 * (h // 2) + 2 * t + h % 2:SUMS + 4 * (h // 2) + 2 * t + h % 2 + 1])
                last.then_inc(*n.up(f"bank{b}_drained"))
            s.run(1 if 1 <= h <= 8 else 0)
            if 1 <= h <= AQ_H:
                empty(("gqa", "t", h - 1), L.attnT[:, (h - 1) % 2, :, :], COLS)
        halves("w_o_attn_2", 0, KD, L.xT[0])
        s.run(8)
        halves("w_out_2", 0, KD, L.xT[0])
        s.run(8)
        s.finish()
        root(2)
        squares(L.x, L.y)
        root(2)
        halves("w_ffn_in_2", 0, KD, L.xT[0])
        s.run(48)
        s.finish()
        load_root()
        s.run(20)
        halves("w_ple_proj_2", 0, 2, L.oT[0])
        s.run(2)
        s.finish()
        root(2)
        s.run(2)
        halves("w_ple_gate_2", 0, KD, L.xT[0])
        s.run(8)
        s.finish()
        root(2)
        squares(L.x, L.y)

    act.wait_ge(L.sems["ident_loaded"], 16)
    act.dma_start(L.const[:, P:CONST_COLS[0]], io["const_first"][:, P:]).then_inc(L.sems["const_loaded"], 16)
    act.wait_ge(L.sems["x_loaded"], 16)
    for g, t in QUARTERS:
        square(L.x[:, t, g * COLS:(g + 1) * COLS], L.y, g, t).then_inc(L.sems["squared"], 1)
    with act.Fori(0, LAYERS) as layer:
        n.enter(FIRST, layer)
        first_layer()
    seg = BETWEEN
    n.enter(BETWEEN, 0)
    act.dma_start(L.const[:, P:CONST_COLS[1]], io["const_second"][:, P:]).then_inc(L.sems["const_loaded"], 16)
    root(2)
    squares(L.x, L.y)
    seg = SECOND
    with act.Fori(0, LAYERS) as layer:
        n.enter(SECOND, layer)
        second_layer()


def vector_program(nc, dve, n, L):
    v = nc.vector
    seg = FIRST
    mix, small, proj, y, x = L.mix, L.small, L.proj, L.y, L.x

    def col(at, w=1):
        return small[:, at:at + w]

    def link(ins, name="dve_step"):
        ins.then_inc(*n.up(name))
        dve.wait_ge(*n.at(name, n.own[name]))

    def tell(name, count=1):
        dve.sem_inc(*n.up(name, count))

    def unit(u):
        pass

    def filled(key):
        b, use = L.banks[seg].get(key)
        dve.wait_ge(*n.at(f"bank{b}_filled", use + 1))
        return b

    def drain(ins, key):
        b, use = L.banks[seg].get(key)
        ins.then_inc(*n.up(f"bank{b}_drained"))
        dve.wait_ge(*n.at(f"bank{b}_drained", use + 1))

    def empty(key, dst, width, rows=P):
        b = filled(key)
        drain(v.tensor_copy(dst, mix[0:rows, b, 0:width]), key)

    def halves(weight, first, k_tiles, dst, at=0):
        if weight in IN_QUARTERS:
            for g, t in QUARTERS:
                b, use = L.banks[seg].get((weight, g, t))
                dve.wait_ge(*n.next("half_ready"))
                hi, lo = (a[:, 4 * g:4 * g + 4, t * P:(t + 1) * P] for a in dst)
                v.tensor_tensor(lo, mix[:, b, :].rearrange("p (k i) -> p k i", k=4), hi.bitcast(F32), ALU.subtract)\
                    .then_inc(*n.up(f"bank{b}_drained"))
            return
        for j in range(0, k_tiles, 2):
            w = min(2, k_tiles - j)
            key = (weight, (first + j) // 2)
            b, use = L.banks[seg].get(key)
            dve.wait_ge(*n.next("half_ready"))
            at_j = slice(at + first + j, at + first + j + w)
            v.tensor_tensor(dst[1][:, at_j, :], mix[:, b, 0:w * TOK].rearrange("p (k t) -> p k t", k=w),
                            dst[0][:, at_j, :].bitcast(F32), ALU.subtract).then_inc(*n.up(f"bank{b}_drained"))

    def refine(width):
        dve.wait_ge(*n.next("root_ready"))
        va, r, a = col(VAR, width), col(ROOT, width), col(NEWTON, width)
        link(v.reciprocal(r, r))
        link(v.tensor_tensor(a, r, r, ALU.mult))
        link(v.scalar_tensor_tensor(out=a, in0=a, scalar=-0.5, in1=va, op0=ALU.mult, op1=ALU.mult))
        link(v.scalar_tensor_tensor(out=r, in0=a, scalar=1.5, in1=r, op0=ALU.add, op1=ALU.mult))

    def mean_square(scratch, rows, out):
        return v.tensor_tensor_reduce(out=scratch, in0=rows, in1=rows, scale=1.0 / rows.shape[-1], scalar=NORM_EPS, op0=ALU.mult, op1=ALU.add, accum_out=out)

    def variance():
        link(v.scalar_tensor_tensor(out=col(VAR, NT), in0=col(PARTS, NT), scalar=NORM_EPS, in1=col(PARTS + NT, NT), op0=ALU.add, op1=ALU.add), "variance")

    def gain_landed(slot):
        dve.wait_ge(*n.dma(f"gain{slot}_loaded", n.own.get(f"gain{slot}_free", 0) + 1))

    def norm_rows(slot, dst, made="rows_ready", opens=False):
        dve.wait_ge(*(n.at("squared", 0) if opens else n.next("squared", 4)))
        variance()
        gain_landed(slot)
        refine(NT)
        for g, t in QUARTERS:
            c = slice(g * COLS, (g + 1) * COLS)
            link(v.scalar_tensor_tensor(out=dst[:, t, c], in0=x[:, t, c], scalar=col(ROOT + t), in1=L.gains[:, slot, c], op0=ALU.mult, op1=ALU.mult), made)
        tell(f"gain{slot}_free")

    def product_times_gains(c):
        gain_landed(1)
        for i in range(len(c.pairs)):
            half = c.to // COLS + i
            cols = slice(half * COLS, (half + 1) * COLS)
            for t in range(NT):
                dve.wait_ge(*n.next("squared"))
                last = v.tensor_tensor(y[:, t, cols], pair(c, i)[:, t], L.gains[:, 1, cols], ALU.mult)
            drained(last, c, i)

    def norm_add(slot, made):
        variance()
        tell(f"gain{slot}_free")
        refine(NT)
        for g, t in QUARTERS:
            c = slice(g * COLS, (g + 1) * COLS)
            link(v.scalar_tensor_tensor(out=x[:, t, c], in0=y[:, t, c], scalar=col(ROOT + t), in1=x[:, t, c], op0=ALU.mult, op1=ALU.add), made)

    def rope(a, b, c, s, shape, scratch=None, apart=512):
        size = int(np.prod(shape))
        names = "xyz"[:len(shape)]
        pat = f"p ({' '.join(names)}) -> p {' '.join(names)}"
        scratch = L.tmp if scratch is None else scratch
        u1, u2 = (scratch[:, i * apart:i * apart + size].rearrange(pat, **dict(zip(names, shape))) for i in range(2))
        v.tensor_tensor(u1, b, s, ALU.mult)
        link(v.tensor_tensor(u2, a, s, ALU.mult))
        v.tensor_tensor(a, a, c, ALU.mult)
        link(v.tensor_tensor(b, b, c, ALU.mult))
        v.tensor_tensor(a, a, u1, ALU.subtract)
        link(v.tensor_tensor(b, b, u2, ALU.add))

    def rope_heads(rows, heads, half, table):
        c, s = (spread(L.cst(f"{k}_{table}", NT, half), 2, heads) for k in "cs")
        rope(rows[:, :, :, 0:half], rows[:, :, :, half:2 * half], c, s, [NT, heads, half])

    def softmax_shift(tag, h, scale):
        s = h % 2
        key = (tag, "s", h)
        b = filled(key)
        tell("step_open")
        for i, c, w in ((0, 0, TOK), (1, TOK, P)):
            last = v.tensor_tensor_reduce(out=L.prob[:, s, c:c + w], in0=mix[:, b, c:c + w], in1=L.cst("causal")[:, c:c + w],
                                   scale=1.0, scalar=-3e38, op0=ALU.add, op1=ALU.max, accum_out=col(MAXIMUM + 2 * s + i))
        drain(last, key)
        v.tensor_scalar(col(SHIFT + 2 * s, 2), col(MAXIMUM + 2 * s, 2), -scale, None, ALU.mult).then_inc(*n.up("shift_ready"))

    def softmax_out(tag, g, base):
        key = (tag, "o", g)
        b = filled(key)
        link(v.reciprocal(col(INVERSE, 8), col(SUMS + 8 * g, 8)))
        inv = spread(col(INVERSE, 8).rearrange("p (t h) -> p t h", t=NT), 3, 64)
        drain(v.tensor_tensor(y[:, :, base:base + 256].rearrange("p t (h d) -> p t h d", h=4),
                              mix[:, b, :].rearrange("p (t h d) -> p t h d", t=NT, h=4), inv, ALU.mult), key)

    def softmax_heads(tag, heads, scale, base, s, units, beside=None):
        for h in range(heads + 2):
            if h < heads:
                softmax_shift(tag, h, scale)
            if beside:
                beside(h)
            if h >= 2 and (h - 2) % 4 == 3:
                softmax_out(tag, (h - 2) // 4, base + (h - 2) // 4 * 256)
            s.run(units[h] if h < len(units) else 0)
        tell("rows_ready")

    def pair(c, i=0):
        return L.acc[:, 2 * c.pairs[i]:2 * c.pairs[i] + 2, :]

    def drained(ins, c, i=0):
        name = f"pair{c.pairs[i]}_drained"
        ins.then_inc(*n.up(name))
        dve.wait_ge(*n.at(name, c.use[i] + 1))

    def read_out(c):
        if c.name == "gate":
            return
        dve.wait_ge(*n.at("unit_used", c.last + 1))
        if c.name == "p":
            drained(v.tensor_copy(proj[:, :, c.to:c.to + c.n], pair(c)[:, :, 0:c.n]), c)
        elif c.name == "q_up":
            drained(v.tensor_copy(y[:, :, c.to:c.to + c.n], pair(c)[:, :, 0:c.n]), c)
        elif c.name == "kv_up":
            heads = pair(c).rearrange("p t (h d) -> p t h d", h=4)
            v.tensor_copy(L.km[:, :, c.to:c.to + 4, 0:NOPE], heads[:, :, :, 0:NOPE])
            drained(v.tensor_copy(L.vm[:, :, c.to:c.to + 4, :], heads[:, :, :, NOPE:]), c)
        elif c.name.startswith("branch"):
            if c.name in ("branch_mla", "branch_moba") and c.col == 0:
                dve.wait_ge(*n.next("gates_ready"))
            g = {"branch_mla": G_MLA, "branch_ret": G_RET, "branch_moba": G_MOBA,
                 "branch_gla": at2(G_A), "branch_attn": at2(G_B)}[c.name] + c.to
            if seg == SECOND:
                gate = next(o for o in L.plans[seg].chunks if o.name == "gate" and o.to == g)
                dve.wait_ge(*n.at(f"pair{gate.pairs[0]}_drained", gate.use[0] + 1))
            drained(v.tensor_tensor(proj[:, :, g:g + COLS], proj[:, :, g:g + COLS], pair(c), ALU.mult), c)
            if c.name not in ("branch_mla", "branch_gla"):
                into = (G_MLA if seg == FIRST else at2(G_A)) + c.to
                m = proj[:, :, into:into + COLS]
                link(v.tensor_tensor(m, m, proj[:, :, g:g + COLS], ALU.add))
            if c.name in ("branch_moba", "branch_attn"):
                tell("rows_ready", NT)
        elif c.name.startswith("residual"):
            for i in range(len(c.pairs)):
                for t in range(NT):
                    r = x[:, t, c.to + i * COLS:c.to + (i + 1) * COLS]
                    link(v.tensor_tensor(r, r, pair(c, i)[:, t], ALU.add), "norm_open")
                tell(f"pair{c.pairs[i]}_drained")
        elif c.name in ("normed", "normed_wide"):
            product_times_gains(c)
        elif c.name == "up":
            slot = (c.to // 4) % 2
            r = y[:, :, slot * COLS:(slot + 1) * COLS]
            drained(v.tensor_scalar(r, pair(c), 0.0, None, ALU.max), c)
            v.tensor_tensor(r, r, r, ALU.mult).then_inc(*n.up("rows_ready"))

        elif c.name == "plain_wide":
            for i in range(2):
                drained(v.tensor_copy(y[:, :, i * COLS:(i + 1) * COLS], pair(c, i)), c, i)
        elif c.name == "glu_gate":
            slot = c.to // 4 % 2
            r = y[:, :, slot * COLS:slot * COLS + c.n]
            dve.wait_ge(*n.next("glu_ready"))
            drained(v.tensor_tensor(r, r, pair(c)[:, :, 0:c.n], ALU.mult), c)
        elif c.name == "ple":
            dve.wait_ge(*n.at(f"pair{c.pairs[0]}_drained", c.use[0] + 1))
            r = y[:, :, c.to:c.to + COLS]
            link(v.tensor_tensor(r, r, proj[:, :, c.to:c.to + COLS], ALU.mult))
            tell("norm_open", NT)
            gain_landed(2)
            dve.wait_ge(*n.next("squared", NT))
            link(v.tensor_tensor(r, r, spread(L.gains[:, 2, c.to:c.to + COLS], 1, NT), ALU.mult))
        elif c.name == "glu_up":
            slot = c.to // 4 % 2
            r = y[:, :, slot * COLS:slot * COLS + c.n]
            drained(v.tensor_tensor(r, r, pair(c)[:, :, 0:c.n], ALU.mult), c)
            tell("rows_ready")

    def hidden(c):
        if c.name == "up" or c.name == "glu_up":
            halves("w_mlp_down" if c.name == "up" else "w_ffn_out_2", c.to, c.n // P, L.hT)

    def retention_out(step):
        o = y[:, :, COLS:2 * COLS]
        oh = [(t, h, y[:, t, COLS + h * RET_V:COLS + (h + 1) * RET_V]) for t in range(NT) for h in range(RET_H)]
        gate = L.tmp[:, :].rearrange("p (t c) -> p t c", t=NT)
        if step == 0:
            for i, (t, h, r) in enumerate(oh):
                last = v.bn_stats(col(STATS + 6 * i, 6), r)
            link(last)
        elif step == 1:
            tell("step_open")
            for i in range(8):
                last = v.bn_aggr(col(MOMENTS + 2 * i, 2), col(STATS + 6 * i, 6))
            link(last)
            v.tensor_scalar(col(VAR, 8), small[:, MOMENTS + 1:MOMENTS + 16:2], GN_EPS, None, ALU.add).then_inc(*n.up("variance"))
        elif step == 2:
            dve.wait_ge(*n.next("silu_ready"))
            link(v.tensor_tensor(gate, gate, proj[:, :, RG:RG + COLS], ALU.mult))
        elif step == 3:
            refine(8)
            for i, (t, h, r) in enumerate(oh):
                last = v.tensor_scalar(r, r, col(MOMENTS + 2 * i), col(ROOT + i), ALU.subtract, ALU.mult)
            link(last)
        elif step in (4, 5):
            gain = spread(L.params[:, 384 + (step - 4) * COLS:384 + (step - 3) * COLS], 1, NT)
            link(v.tensor_tensor(o, o, gain, (ALU.mult, ALU.add)[step - 4]))
        elif step == 6:
            tell("params_free")
            link(v.tensor_tensor(o, o, gate, ALU.mult))
            tell("rows_ready")

    def first_layer():
        s = Stream(L.plans[FIRST], unit, [(EVAC, read_out), (TURN, hidden)])
        norm_rows(0, y, opens=True)
        halves("w_in", 0, KD, L.xT)
        s.run(6)
        dve.wait_ge(L.sems["const_loaded"], 16)
        dve.wait_ge(*n.dma("params_loaded", 4))
        for i, (a, w) in enumerate(((CQ, MLA_Q), (CKV, MLA_KV))):
            for t in range(NT):
                last = mean_square(L.tmp[:, (2 * i + t) * 256:(2 * i + t) * 256 + w], proj[:, t, a:a + w], col(VAR + 2 * i + t))
        link(last)
        tell("variance")
        rope_heads(proj[:, :, KR:KR + ROPE].rearrange("p t (h d) -> p t h d", h=1), 1, ROPE // 2, "mla")
        s.run(4)
        refine(4)
        for i, (a, w, g) in enumerate(((CQ, MLA_Q, 0), (CKV, MLA_KV, MLA_Q))):
            for t in range(NT):
                r = proj[:, t, a:a + w]
                last = v.scalar_tensor_tensor(out=r, in0=r, scalar=col(ROOT + 2 * i + t), in1=L.params[:, g:g + w], op0=ALU.mult, op1=ALU.mult)
        last.then_inc(*n.up("rows_ready"))
        halves("mla_w_q_up", 0, 2, L.oT)
        halves("mla_w_kv_up", 0, 1, L.oT, 2)
        v.tensor_copy(L.km[:, :, :, NOPE:], spread(proj[:, :, KR:KR + ROPE], 2, MLA_H))
        s.run(20)
        rope_heads(proj[:, :, MQ:MV].rearrange("p t (h d) -> p t h d", d=MOBA_D), 2 * MOBA_H, MOBA_R // 2, "moba")
        s.run(3)
        s.run(1)
        rope_heads(y[:, :, 0:MLA_H * QK_D].rearrange("p t (h d) -> p t h d", d=QK_D)[:, :, :, NOPE:], MLA_H, ROPE // 2, "mla")
        tell("rows_ready")
        for j in range(4):
            empty(("mla", "k", j), L.kT[0:QK_D, 2 * j:2 * j + 2, :], 2 * TOK, QK_D)
        rope_heads(proj[:, :, RQ:RV].rearrange("p t (h d) -> p t h d", d=RET_K), 2 * RET_H, RET_K // 2, "ret")
        tell("rotated")
        softmax_heads("mla", MLA_H, QK_D ** -0.5, 0, s, [2, 2, 1, 2, 1, 2, 1, 2, 1, 0])
        tell("rows_ready")
        empty(("ret", "k", 0), L.kT[:, 0:2, :], 2 * TOK)
        halves("w_branch_mla", 0, 4, L.oT)
        for h in range(RET_H + 1):
            if h < RET_H:
                key = ("ret", "s", h)
                b = filled(key)
                drain(v.tensor_tensor(L.probT[:, h % 2, :], mix[:, b, 0:384], L.cst("decay", RET_H, 384)[:, h], ALU.mult), key)
            s.run(1 if h else 0)
            if h in (2, 4):
                g = h // 2 - 1
                key = ("ret", "o", g)
                b = filled(key)
                drain(v.tensor_copy(y[:, :, COLS + g * 256:COLS + (g + 1) * 256], mix[:, b, :].rearrange("p (t c) -> p t c", t=NT)), key)
        for j in range(2):
            empty(("moba", "k", j), L.kT[:, 2 * j:2 * j + 2, :], 2 * TOK)
        softmax_heads("moba", MOBA_H, MOBA_D ** -0.5, 0, s, [1, 1, 1, 1, 1, 1, 1, 1, 0, 0], retention_out)
        halves("w_branch_ret", 0, 4, L.oT)
        s.run(4)
        halves("w_branch_moba", 0, 4, L.oT)
        s.run(4)
        s.finish()
        halves("w_out", 0, KD, L.xT)
        s.run(8)
        s.finish()
        norm_rows(1, y)
        halves("w_mlp_up", 0, KD, L.xT)
        s.run(32)
        s.finish()
        s.run(32)
        s.finish()

    def gla_states(h):
        for d in range(2):
            for i in range(3):
                c = i if d == 0 else 3 - i
                j = next(j for j, pairs in enumerate(KV_BANKS) if (d, c) in pairs)
                m = KV_BANKS[j].index((d, c))
                key = ("gla", "kv", h, j)
                b = filled(key)
                kv = mix[:, b, m * GLA_V:(m + 1) * GLA_V]
                if i == 0:
                    ins = v.tensor_copy(L.states[:, d, 0, :], kv)
                else:
                    ins = v.scalar_tensor_tensor(out=L.states[:, d, i, :], in0=L.states[:, d, i - 1, :],
                                                 scalar=col(LASTS + 16 * d + 4 * h + c), in1=kv, op0=ALU.mult, op1=ALU.add)
                if m == len(KV_BANKS[j]) - 1:
                    drain(ins, key)
                else:
                    link(ins)
        tell("states_ready")

    def query_norms(first, end):
        rows = [(h, proj[:, t, at2(AQ) + h * A_D:at2(AQ) + (h + 1) * A_D]) for h in range(first, end) for t in range(NT)]
        for i, (h, r) in enumerate(rows):
            last = mean_square(L.tmp[:, i % 8 * A_D:(i % 8 + 1) * A_D], r, col(VAR + i))
            if i % 8 == 7:
                link(last)
        if len(rows) % 8:
            link(last)
        tell("variance")
        refine(len(rows))
        for i, (h, r) in enumerate(rows):
            w = GLA_V if h < AQ_H else GLA_V + A_D
            last = v.scalar_tensor_tensor(out=r, in0=r, scalar=col(ROOT + i), in1=L.params[:, w:w + A_D], op0=ALU.mult, op1=ALU.mult)
        link(last)

    def query_rope(first, end):
        for t in range(NT):
            r = proj[:, t, at2(AQ) + first * A_D:at2(AQ) + end * A_D].rearrange("p (h a s d) -> p h a s d", a=2, s=2, d=A_D // 4)
            c, sn = (spread(L.cst(f"{w}_ax", NT, 64)[:, t].rearrange("p (a d) -> p a d", a=2), 1, end - first) for w in "cs")
            rope(r[:, :, :, 0, :], r[:, :, :, 1, :], c, sn, [end - first, 2, A_D // 4], L.tmp)

    def second_layer():
        s = Stream(L.plans[SECOND], unit, [(EVAC, read_out), (TURN, hidden)])
        norm_rows(0, y, opens=True)
        halves("w_in_2", 0, KD, L.xT)
        s.run(14)
        tell("rows_ready")
        s.run(2)
        dve.wait_ge(*n.dma("params_loaded", 4))
        for d in range(2):
            la = y[:, :, d * COLS:(d + 1) * COLS]
            bias = L.params[:, COLS * (d + 1):COLS * (d + 2)]
            for t in range(NT):
                key = ("gla", "z", d, t)
                b = filled(key)
                drain(v.tensor_tensor(la[:, t], mix[:, b, :], bias, ALU.add), key)
            link(v.scalar_tensor_tensor(out=L.soft[:, d], in0=la, scalar=-1.0, in1=la, op0=ALU.mult, op1=ALU.min), "minus_abs")
        for d in range(2):
            la = y[:, :, d * COLS:(d + 1) * COLS]
            link(v.tensor_scalar(la, la, 0.0, None, ALU.min))
        for d in range(2):
            la = y[:, :, d * COLS:(d + 1) * COLS]
            dve.wait_ge(*n.next("softplus"))
            link(v.tensor_tensor(la, la, L.soft[:, d], ALU.subtract), "decays_ready")
        s.run(4)
        for d in range(2):
            b, use = L.banks[seg].get(("gla", "last", d))
            dve.wait_ge(*n.at(f"bank{b}_drained", use + 1))
            gq, gk = proj[:, :, GQ:GQ + COLS], proj[:, :, GK:GK + COLS]
            v.scalar_tensor_tensor(out=L.qd[:, :, :], in0=L.qd[:, :, :], scalar=GLA_K ** -0.5, in1=gq, op0=ALU.mult, op1=ALU.mult)
            link(v.tensor_tensor(L.kd[:, :, :], L.kd[:, :, :], gk, ALU.mult))
            tell("rows_ready")
            link(v.tensor_tensor(L.ks[:, d], L.ks[:, d], gk, ALU.mult))
            s.run(3)
            for j in range(2):
                empty(("gla", "k", d, j), L.kT[:, 4 * d + 2 * j:4 * d + 2 * j + 2, :], 2 * TOK)
            s.run(2)
        for h in range(GLA_H):
            key = ("gla", "s", h)
            b = filled(key)
            for d in range(2):
                mask = spread(L.cst("in_" + "fb"[d]), 1, NT)
                last = v.tensor_tensor(L.seenT[:, h % 2, d], mix[:, b, d * TOK:(d + 1) * TOK].rearrange("p (t i) -> p t i", t=NT), mask, ALU.mult)
            drain(last, key)
            gla_states(h)
            if h == 1:
                query_norms(0, 4)
            elif h == 2:
                query_rope(0, 4)
            s.run(2)
            s.run(1)
        tell("gg_ready")
        b, use = L.banks[seg].get(("gla", "o", GLA_H - 1))
        dve.wait_ge(*n.at(f"bank{b}_drained", use + 1))
        oh = [y[:, t, h * GLA_V:(h + 1) * GLA_V] for t in range(NT) for h in range(GLA_H)]
        for i, r in enumerate(oh):
            last = mean_square(L.wide[:, i * GLA_V:(i + 1) * GLA_V], r, col(VAR + i))
        link(last)
        tell("variance")
        refine(8)
        for i, r in enumerate(oh):
            last = v.scalar_tensor_tensor(out=r, in0=r, scalar=col(ROOT + i), in1=L.params[:, 0:GLA_V], op0=ALU.mult, op1=ALU.mult)
        link(last)
        dve.wait_ge(*n.next("silu_ready"))
        g = L.silu[:, :, :]
        link(v.tensor_tensor(g, g, proj[:, :, at2(GG):at2(GG) + D], ALU.mult))
        for half in range(2):
            c = slice(half * COLS, (half + 1) * COLS)
            link(v.tensor_tensor(y[:, :, c], y[:, :, c], g[:, :, c], ALU.mult))
            tell("rows_ready", NT)
        query_norms(4, AQ_H + AKV_H)
        tell("params_free")
        query_rope(4, AQ_H + AKV_H)
        tell("walpha_used")
        s.run(14)
        tell("rows_ready")
        halves("w_o_gla_2", 0, KD, L.xT)
        empty(("gqa", "k", 0), L.kT[:, 0:2, :], 2 * TOK)
        for h in range(AQ_H + 2):
            if h < AQ_H:
                b = filled(("gqa", "s", h))
                m = 2 * (h % 2)
                link(v.tensor_reduce(col(MAXIMUM + m, 2), mix[:, b, :].rearrange("p (t k) -> p t k", t=NT), AX.X, ALU.max))
                v.tensor_scalar(col(SHIFT + m, 2), col(MAXIMUM + m, 2), -(A_D ** -0.5), None, ALU.mult).then_inc(*n.up("shift_ready"))
            if h >= 3 and h % 2 == 1:
                g = (h - 3) // 2
                key = ("gqa", "o", g)
                b = filled(key)
                link(v.reciprocal(col(INVERSE, 4), col(SUMS + 4 * g, 4)))
                inv = spread(col(INVERSE, 4).rearrange("p (t h) -> p t h", t=NT), 3, A_D)
                drain(v.tensor_tensor(y[:, :, g * 256:(g + 1) * 256].rearrange("p t (h d) -> p t h d", h=2),
                                      mix[:, b, :].rearrange("p (t h d) -> p t h d", t=NT, h=2), inv, ALU.mult), key)
                if g % 2:
                    tell("rows_ready", NT)
            s.run(1 if 1 <= h <= 8 else 0)
        tell("heads_done")
        halves("w_o_attn_2", 0, KD, L.xT)
        s.run(8)
        s.finish()
        halves("w_out_2", 0, KD, L.xT)
        s.run(8)
        s.finish()
        norm_add(1, "norm_open")
        norm_rows(0, y)
        halves("w_ffn_in_2", 0, KD, L.xT)
        s.run(48)
        s.finish()
        s.run(20)
        halves("w_ple_proj_2", 0, 2, L.oT)
        s.run(2)
        s.finish()
        norm_add(1, "rows_ready")
        s.run(2)
        halves("w_ple_gate_2", 0, KD, L.xT)
        s.run(8)
        s.finish()
        norm_add(2, "norm_open")

    for b in range(4):
        dve.sem_inc(L.sems[f"bank{b}_drained"], 1)
    for name in ("pair0_drained", "pair1_drained", "gain0_free", "gain1_free", "gain2_free", "params_free"):
        dve.sem_inc(L.sems[name], 1)
    for slot in range(RING):
        last = v.memset(L.raw[:, slot], 0.0)
    last.then_inc(L.sems["ring_clear"], 1)
    dve.wait_ge(L.sems["x_loaded"], 16)
    with dve.Fori(0, LAYERS) as layer:
        n.enter(FIRST, layer)
        first_layer()
    seg = BETWEEN
    n.enter(BETWEEN, 0)
    norm_rows(2, x, "norm_open", opens=True)
    dve.sem_inc(L.sems["walpha_used"], 1)
    seg = SECOND
    dve.wait_ge(L.sems["const_loaded"], 32)
    with dve.Fori(0, LAYERS) as layer:
        n.enter(SECOND, layer)
        second_layer()
    dve.sem_inc(L.sems["result_ready"], 1)



INPUTS = ['x', 'attn_norm', 'w_in', 'mla_q_norm', 'mla_kv_norm', 'mla_w_q_up', 'mla_w_kv_up', 'ret_gn_w', 'ret_gn_b',
 'w_branch_mla', 'w_branch_moba', 'w_branch_ret', 'w_out', 'mlp_norm', 'w_mlp_up', 'w_mlp_down', 'final_norm',
 'p_2', 'g_mix_pre_2', 'w_in_2', 'w_alpha_up_2', 'b_alpha_2', 'g_gla_out_2', 'g_q_norm_2', 'g_k_norm_2',
 'w_o_gla_2', 'w_o_attn_2', 'w_out_2', 'g_mix_post_2', 'g_ffn_pre_2', 'w_ffn_in_2', 'w_ffn_out_2',
 'g_ffn_post_2', 'w_ple_proj_2', 'w_ple_gate_2', 'g_ple_post_2']


def kernel(**inputs):
    import concourse.bacc as bacc
    from concourse.bass_utils import run_bass_kernel_spmd

    nc = bacc.Bacc("TRN2", target_bir_lowering=False, num_devices=1)
    arrays = {name: np.ascontiguousarray(inputs[name]) for name in INPUTS}
    arrays["const_first"], arrays["const_second"] = constants()
    io = {name: nc.dram_tensor(f"in_{name}", a.shape, F32, kind="ExternalInput").ap() for name, a in arrays.items()}
    io["out"] = nc.dram_tensor("out_0", (1, TOK, D), F32, kind="ExternalOutput").ap()
    sent = {name: [0, 0, 0] for name in SIGNALS}
    build(nc, io, SIGNALS, sent)
    assert sent == SIGNALS, "the table of signals doesn't fit the program"
    result = run_bass_kernel_spmd(nc, [{f"in_{name}": a for name, a in arrays.items()}], core_ids=[0])
    return result.results[0]["out_0"]
```
